# Optimizing a Trainium2 kernel written in Bass

```python
import jax, jax.numpy as jnp
from jax import lax
import numpy as np

D_MODEL = 1024
BATCH = 1
SEQ = 256
DEPTH = 1

GRID_W = 64
CTX_LEN = 256

HEAD_DIM = 64
RWKV_WIDTH = D_MODEL
RWKV_HEADS = RWKV_WIDTH // HEAD_DIM
DECAY_LORA = 64
ICLR_LORA = 64
GATE_LORA = 128
GN_EPS = 64e-5
NORM_EPS = 1e-12
CONV_WIDTH = D_MODEL
CONV_GROUPS = CONV_WIDTH // HEAD_DIM
CONV_K = 3
N_EXPERTS = 32
TOP_K = 4
D_FF = D_MODEL
SWIGLU_LIMIT = 7.0
SWIGLU_ALPHA = 1.702
MOE_BLOCK = 256
RMS_EPS = 1e-6

K_OFF = 0
V_OFF = K_OFF + RWKV_WIDTH
DECAY_OFF = V_OFF + RWKV_WIDTH
ICLR_OFF = DECAY_OFF + 2 * DECAY_LORA
STATE_COLS = ICLR_OFF + 2 * ICLR_LORA
R_OFF = STATE_COLS
GLORA_OFF = R_OFF + RWKV_WIDTH
SHIFT_COLS = GLORA_OFF + GATE_LORA
CONV_OFF = SHIFT_COLS
GATE_OFF = CONV_OFF + 3 * CONV_WIDTH
N_IN = GATE_OFF + 2 * D_MODEL

kernel_name = 'hybrid_rwkv7_shortconv_moe_diffusion_block'

def _rmsnorm(x, g):
    xf = x.astype(jnp.float32)
    y = xf * lax.rsqrt(jnp.mean(xf * xf, axis=-1, keepdims=True) + RMS_EPS)
    return (y * g.astype(jnp.float32)).astype(x.dtype)

def _shift(z, axis, step):
    n = z.shape[axis]
    pad = [(0, 0)] * z.ndim
    if step > 0:
        body = lax.slice_in_dim(z, 0, n - step, axis=axis)
        pad[axis] = (step, 0)
    else:
        body = lax.slice_in_dim(z, -step, n, axis=axis)
        pad[axis] = (0, -step)
    return jnp.pad(body, pad)

def _qshift_grid(z, mu):
    b, t, ch = z.shape
    rows = t // GRID_W
    zg = z.reshape(b, rows, GRID_W, ch // 4, 4)
    shifted = jnp.stack([
        _shift(zg[..., 0], 2, 1),
        _shift(zg[..., 1], 2, -1),
        _shift(zg[..., 2], 1, 1),
        _shift(zg[..., 3], 1, -1),
    ], axis=-1).reshape(b, t, ch)
    return z + mu * (shifted - z)

def _qshift_seq(z, mu):
    b, t, ch = z.shape
    zg = z.reshape(b, t, ch // 4, 4)
    shifted = jnp.stack([
        _shift(zg[..., 0], 1, 1),
        _shift(zg[..., 1], 1, -1),
        _shift(zg[..., 2], 1, 1),
        _shift(zg[..., 3], 1, -1),
    ], axis=-1).reshape(b, t, ch)
    return z + mu * (shifted - z)

def _heads(u):
    return u.reshape(u.shape[0], u.shape[1], RWKV_HEADS, HEAD_DIM).astype(jnp.float32)

def _rwkv_state_terms(zs, w0, w_decay_up, a0, w_iclr_up, k_k, k_a):
    f32 = jnp.float32
    k = zs[..., K_OFF:K_OFF + RWKV_WIDTH]
    v = zs[..., V_OFF:V_OFF + RWKV_WIDTH]
    kk = _heads(k * k_k)
    kk = kk / jnp.maximum(jnp.sqrt(jnp.sum(kk * kk, axis=-1, keepdims=True)), NORM_EPS)
    dirs = []
    for d in range(2):
        lw = zs[..., DECAY_OFF + d * DECAY_LORA:DECAY_OFF + (d + 1) * DECAY_LORA]
        la = zs[..., ICLR_OFF + d * ICLR_LORA:ICLR_OFF + (d + 1) * ICLR_LORA]
        w_log = -jax.nn.softplus(-(w0[d] + jnp.tanh(lw) @ w_decay_up[d]).astype(f32)) - 0.5
        decay = jnp.exp(-jnp.exp(w_log))
        a = jax.nn.sigmoid((a0[d] + la @ w_iclr_up[d]).astype(f32))
        k_dir = k.astype(f32) * (1.0 + (a - 1.0) * k_a.astype(f32))
        dirs.append((_heads(decay), _heads(k_dir), kk * _heads(a)))
    return _heads(v), kk, dirs

def _wkv_scan(s0, decay, k, v, kk, kka, r, reverse):
    seq = [decay, k, v, kk, kka] + ([] if r is None else [r])
    xs = tuple(jnp.moveaxis(u, 1, 0) for u in seq)

    def step(s, inp):
        w_t, k_t, v_t, kk_t, kka_t = inp[:5]
        sa = jnp.einsum('bhvk,bhk->bhv', s, kk_t)
        s = (s * w_t[:, :, None, :] - sa[..., None] * kka_t[:, :, None, :]
             + v_t[..., None] * k_t[:, :, None, :])
        y = jnp.einsum('bhvk,bhk->bhv', s, inp[5]) if len(inp) == 6 else None
        return s, y

    s_fin, ys = lax.scan(step, s0, xs, reverse=reverse)
    return s_fin, (None if r is None else jnp.moveaxis(ys, 0, 1))

def _conv3(u, w):
    return lax.conv_general_dilated(
        u, w[:, None, :].astype(u.dtype), window_strides=(1,), padding=((1, 1),),
        dimension_numbers=('NWC', 'WIO', 'NWC'), feature_group_count=u.shape[-1])

def _merge_branches(z, r, lg, y, k_bonus, v, r_k, ln_x_w, ln_x_b, w_gate_up, conv_w, w_out):
    b, t, _ = z.shape
    mean = jnp.mean(y, axis=-1, keepdims=True)
    var = jnp.mean(jnp.square(y - mean), axis=-1, keepdims=True)
    yn = ((y - mean) * lax.rsqrt(var + GN_EPS)).reshape(b, t, RWKV_WIDTH) * ln_x_w + ln_x_b
    bonus = (jnp.sum(r * k_bonus * r_k, axis=-1, keepdims=True) * v).reshape(b, t, RWKV_WIDTH)
    g = jax.nn.sigmoid(lg) @ w_gate_up
    y_rwkv = ((yn + bonus) * g).astype(z.dtype)
    gb = z[..., CONV_OFF:CONV_OFF + CONV_WIDTH]
    gc = z[..., CONV_OFF + CONV_WIDTH:CONV_OFF + 2 * CONV_WIDTH]
    xin = z[..., CONV_OFF + 2 * CONV_WIDTH:CONV_OFF + 3 * CONV_WIDTH]
    y_conv = gb * _conv3(gc * xin, conv_w)
    ga = z[..., GATE_OFF:GATE_OFF + D_MODEL]
    gbr = z[..., GATE_OFF + D_MODEL:GATE_OFF + 2 * D_MODEL]
    merged = jax.nn.sigmoid(ga) * y_rwkv + jax.nn.sigmoid(gbr) * y_conv
    return merged @ w_out

def _moe(h, w_router, b_router, w_exp_in, b_exp_in, w_exp_out, b_exp_out):
    n, d = h.shape
    logits = (h @ w_router + b_router).astype(jnp.float32)
    top_val, top_idx = lax.top_k(logits, TOP_K)
    gates = jax.nn.softmax(top_val, axis=-1)
    nk = n * TOP_K
    flat_e = top_idx.reshape(-1).astype(jnp.int32)
    flat_tok = jnp.arange(nk, dtype=jnp.int32) // TOP_K
    flat_g = gates.reshape(-1)
    order = jnp.argsort(flat_e)
    e_sorted, tok_sorted, g_sorted = flat_e[order], flat_tok[order], flat_g[order]
    counts = jnp.bincount(flat_e, length=N_EXPERTS).astype(jnp.int32)
    starts = jnp.cumsum(counts) - counts
    padded = (counts + MOE_BLOCK - 1) // MOE_BLOCK * MOE_BLOCK
    pad_ends = jnp.cumsum(padded)
    pad_starts = pad_ends - padded
    dest = pad_starts[e_sorted] + jnp.arange(nk, dtype=jnp.int32) - starts[e_sorted]
    n_blocks = -(-(nk + N_EXPERTS * (MOE_BLOCK - 1)) // MOE_BLOCK)
    n_rows = n_blocks * MOE_BLOCK
    row_tok = jnp.zeros((n_rows,), jnp.int32).at[dest].set(tok_sorted)
    row_g = jnp.zeros((n_rows,), jnp.float32).at[dest].set(g_sorted)
    block_e = jnp.minimum(
        jnp.searchsorted(pad_ends, jnp.arange(n_blocks, dtype=jnp.int32) * MOE_BLOCK, side='right'),
        N_EXPERTS - 1)
    xb = h[row_tok].reshape(n_blocks, MOE_BLOCK, d)

    def expert_block(args):
        xblk, e = args
        gu = xblk @ w_exp_in[e] + b_exp_in[e]
        gate = jnp.minimum(gu[:, :D_FF], SWIGLU_LIMIT)
        up = jnp.clip(gu[:, D_FF:], -SWIGLU_LIMIT, SWIGLU_LIMIT)
        act = (up + 1.0) * gate * jax.nn.sigmoid(SWIGLU_ALPHA * gate)
        return act @ w_exp_out[e] + b_exp_out[e]

    yb = lax.map(expert_block, (xb, block_e)).reshape(n_rows, d)
    return jax.ops.segment_sum(yb * row_g[:, None].astype(yb.dtype), row_tok, num_segments=n)

def setup_inputs(seed: int = 0) -> dict:
    key = jax.random.key(seed)
    ks = jax.random.split(key, 30)
    f32 = jnp.float32
    L, D = DEPTH, D_MODEL

    def nrm(i, shape, scale):
        return jax.random.normal(ks[i], shape, f32) * scale

    def unif(i, shape, lo, hi):
        return jax.random.uniform(ks[i], shape, f32, lo, hi)

    return {
        'x': nrm(0, (BATCH, SEQ, D), 1.0),
        'c': nrm(1, (BATCH, D), 1.0),
        'ctx': nrm(2, (BATCH, CTX_LEN, D), 1.0),
        'c_ctx': nrm(3, (D,), 1.0),
        'w_ada': nrm(4, (L, D, 6 * D), 0.5 * D ** -0.5),
        'b_ada': nrm(5, (L, 6 * D), 0.01),
        'norm_pre_mix': 1.0 + nrm(6, (L, D), 0.02),
        'norm_post_mix': 1.0 + nrm(7, (L, D), 0.02),
        'norm_pre_ffn': 1.0 + nrm(8, (L, D), 0.02),
        'norm_post_ffn': 1.0 + nrm(9, (L, D), 0.02),
        'w_in': nrm(10, (L, D, N_IN), D ** -0.5),
        'mu_shift': unif(11, (L, SHIFT_COLS), 0.0, 0.5),
        'w0': unif(12, (L, 2, RWKV_WIDTH), -6.0, -1.0),
        'w_decay_up': nrm(13, (L, 2, DECAY_LORA, RWKV_WIDTH), 0.1),
        'a0': nrm(14, (L, 2, RWKV_WIDTH), 0.1),
        'w_iclr_up': nrm(15, (L, 2, ICLR_LORA, RWKV_WIDTH), ICLR_LORA ** -0.5),
        'k_k': 0.85 + nrm(16, (L, RWKV_WIDTH), 0.05),
        'k_a': 1.0 + nrm(17, (L, RWKV_WIDTH), 0.05),
        'r_k': nrm(18, (L, RWKV_HEADS, HEAD_DIM), 0.1),
        'w_gate_up': nrm(19, (L, GATE_LORA, RWKV_WIDTH), GATE_LORA ** -0.5),
        'ln_x_w': 1.0 + nrm(20, (L, RWKV_WIDTH), 0.02),
        'ln_x_b': nrm(21, (L, RWKV_WIDTH), 0.01),
        'conv_w': nrm(22, (L, CONV_K, CONV_WIDTH), CONV_K ** -0.5),
        'w_out': nrm(23, (L, D, D), D ** -0.5),
        'w_router': nrm(24, (L, D, N_EXPERTS), D ** -0.5),
        'b_router': nrm(25, (L, N_EXPERTS), 0.01),
        'w_exp_in': nrm(26, (L, N_EXPERTS, D, 2 * D_FF), D ** -0.5),
        'b_exp_in': nrm(27, (L, N_EXPERTS, 2 * D_FF), 0.01),
        'w_exp_out': nrm(28, (L, N_EXPERTS, D_FF, D), D_FF ** -0.5),
        'b_exp_out': nrm(29, (L, N_EXPERTS, D), 0.01),
    }

def reference(x, c, ctx, c_ctx, w_ada, b_ada, norm_pre_mix, norm_post_mix, norm_pre_ffn, norm_post_ffn,
              w_in, mu_shift, w0, w_decay_up, a0, w_iclr_up, k_k, k_a, r_k, w_gate_up, ln_x_w, ln_x_b,
              conv_w, w_out, w_router, b_router, w_exp_in, b_exp_in, w_exp_out, b_exp_out):
    xc = ctx
    b = x.shape[0]
    for l in range(DEPTH):
        last = l == DEPTH - 1
        mod = jax.nn.silu(c) @ w_ada[l] + b_ada[l]
        mod_c = jax.nn.silu(c_ctx) @ w_ada[l] + b_ada[l]
        sh1, sc1, g1, sh2, sc2, g2 = jnp.split(mod[:, None, :], 6, axis=-1)
        csh1, csc1, cg1, csh2, csc2, cg2 = jnp.split(mod_c, 6)
        rw_state = (w0[l], w_decay_up[l], a0[l], w_iclr_up[l], k_k[l], k_a[l])
        rw_read = (r_k[l], ln_x_w[l], ln_x_b[l], w_gate_up[l], conv_w[l], w_out[l])

        h = _rmsnorm(x, norm_pre_mix[l]) * (1.0 + sc1) + sh1
        hc = _rmsnorm(xc, norm_pre_mix[l]) * (1.0 + csc1) + csh1
        z = h @ w_in[l]
        zs = _qshift_grid(z[..., :SHIFT_COLS], mu_shift[l])
        n_ctx = STATE_COLS if last else N_IN
        n_ctx_shift = STATE_COLS if last else SHIFT_COLS
        zc = hc @ w_in[l][:, :n_ctx]
        zcs = _qshift_seq(zc[..., :n_ctx_shift], mu_shift[l][:n_ctx_shift])

        v, kk, dirs = _rwkv_state_terms(zs[..., :STATE_COLS], *rw_state)
        vc, kkc, dirs_c = _rwkv_state_terms(zcs[..., :STATE_COLS], *rw_state)
        r = _heads(zs[..., R_OFF:R_OFF + RWKV_WIDTH])
        rc = None if last else _heads(zcs[..., R_OFF:R_OFF + RWKV_WIDTH])
        s0 = jnp.zeros((b, RWKV_HEADS, HEAD_DIM, HEAD_DIM), jnp.float32)
        y_dirs, yc_dirs = [], []
        for d in range(2):
            dec_c, k_c, kka_c = dirs_c[d]
            s_ctx, yc_d = _wkv_scan(s0, dec_c, k_c, vc, kkc, kka_c, rc, d == 1)
            dec, k_d, kka = dirs[d]
            _, y_d = _wkv_scan(s_ctx, dec, k_d, v, kk, kka, r, d == 1)
            y_dirs.append(y_d)
            yc_dirs.append(yc_d)
        y = y_dirs[0] + y_dirs[1]
        k_bonus = 0.5 * (dirs[0][1] + dirs[1][1])
        mix = _merge_branches(z, r, zs[..., GLORA_OFF:SHIFT_COLS], y, k_bonus, v, *rw_read)
        x = x + g1 * _rmsnorm(mix, norm_post_mix[l])
        if not last:
            yc = yc_dirs[0] + yc_dirs[1]
            kc_bonus = 0.5 * (dirs_c[0][1] + dirs_c[1][1])
            mix_c = _merge_branches(zc, rc, zcs[..., GLORA_OFF:SHIFT_COLS], yc, kc_bonus, vc, *rw_read)
            xc = xc + cg1 * _rmsnorm(mix_c, norm_post_mix[l])

        moe_p = (w_router[l], b_router[l], w_exp_in[l], b_exp_in[l], w_exp_out[l], b_exp_out[l])
        h2 = (_rmsnorm(x, norm_pre_ffn[l]) * (1.0 + sc2) + sh2).reshape(-1, D_MODEL)
        if last:
            f = _moe(h2, *moe_p)
        else:
            h2c = (_rmsnorm(xc, norm_pre_ffn[l]) * (1.0 + csc2) + csh2).reshape(-1, D_MODEL)
            f_all = _moe(jnp.concatenate([h2, h2c], axis=0), *moe_p)
            f = f_all[:h2.shape[0]]
            xc = xc + cg2 * _rmsnorm(f_all[h2.shape[0]:].reshape(xc.shape), norm_post_ffn[l])
        x = x + g2 * _rmsnorm(f.reshape(x.shape), norm_post_ffn[l])
    return x


_drawn_inputs = setup_inputs


def setup_inputs(seed=0):
    import zlib

    import numpy as np

    out = dict(_drawn_inputs(seed))
    spreads = {}
    factors = {'norm_post_mix': 3.125,
     'norm_post_ffn': 8.0,
     'a0': 3.034,
     'k_k': 3.014,
     'k_a': 2.86,
     'ln_x_w': 3.291,
     'ln_x_b': 5.003,
     'b_router': 3.114,
     'b_exp_in': 8.0,
     'b_exp_out': 8.0}
    for name, (base, spread) in spreads.items():
        noise = np.random.default_rng([zlib.crc32(name.encode()), seed]).standard_normal(out[name].shape)
        drawn = base * np.exp(spread * noise) if base else spread * noise
        out[name] = __import__('jax').numpy.asarray(drawn.astype(out[name].dtype))
    for name, factor in factors.items():
        out[name] = (out[name] * factor).astype(out[name].dtype)
    return out
```

```python
from contextlib import ExitStack, contextmanager

import numpy as np

import concourse.bass as bass
from concourse import mybir

F32 = mybir.dt.float32
F32R = mybir.dt.float32r
I32 = mybir.dt.int32
ALU = mybir.AluOpType
ACT = mybir.ActivationFunctionType
AX = mybir.AxisListType.X

P = 128
D = 1024
KT = D // P
NTOK = 256
T = 2 * NTOK
TT = NTOK // P
GRID_W = 64
C = 64
NC = T // C
NL = NC // 2
NE = 32
TOPK = 4
FF = D
LORA = 64
EPS = 1e-6
GN_EPS = 64e-5
BLK = 32
DECAY_C = -0.5 * float(np.exp(-0.5))
BIG = 1.0e6

K_OFF, V_OFF, DEC_OFF, ICL_OFF, R_OFF, GL_OFF = 0, 1024, 2048, 2176, 2304, 3328
GB_OFF, GC_OFF, XIN_OFF, GA_OFF, GBR_OFF = 3456, 4480, 5504, 6528, 7552
SHARED = [DEC_OFF, ICL_OFF, GL_OFF]
PER_TILE = [K_OFF, V_OFF, R_OFF, GA_OFF, GBR_OFF, GB_OFF, GC_OFF, XIN_OFF]
NSLOT = len(PER_TILE)

HOST_PAR = ["mu_k", "mu_v", "mu_r", "w0_0", "w0_1", "a0_0", "a0_1", "k_k", "k_a", "r_k", "ln_w", "ln_b",
            "cw0", "cw1", "cw2", "npm"]
DERIVED = ["hw0_0", "hw0_1", "ha0_0", "ha0_1", "hka", "omka", "hrk"]
MIX = ["om", "q0", "q1", "q2", "q3", "prev", "next"]
PAR = {n: i for i, n in enumerate(HOST_PAR + DERIVED + [f"{m}_{t}" for t in "kvr" for m in MIX])}
NHOST, NPAR = len(HOST_PAR), len(PAR)

CONST = {}
_n = 0
for _name, _w in (("ident", P), ("ones", P), ("heads", P), ("headmean", P), ("before", P), ("slots", P),
                  ("cls", 4), ("scan0", T), ("scan1", T),
                  *((f"{m}{d}", C) for d in (0, 1) for m in ("nF", "eF", "nP", "sF", "iF"))):
    CONST[_name] = (_n, _w)
    _n += _w
NCONST = _n


def constants():
    out = np.zeros((P, NCONST), np.float32)

    def put(name, a):
        o, w = CONST[name]
        out[:, o:o + w] = a

    p = np.arange(P)
    put("ident", np.eye(P))
    put("ones", 1.0)
    same = (p[:, None] // C == p[None] // C).astype(np.float32)
    put("heads", same)
    put("headmean", same / C)
    put("before", (p[:, None] < p[None]).astype(np.float32))
    put("slots", np.broadcast_to(p, (P, P)))
    put("cls", (p[:, None] % 4 == np.arange(4)).astype(np.float32))
    t = np.arange(T)
    put("scan0", (t % C != 0).astype(np.float32)[None])
    put("scan1", (t % C != C - 1).astype(np.float32)[None])
    s, u = (p % C)[:, None], np.arange(C)[None]
    block = s // BLK == u // BLK
    for d in (0, 1):
        later = u > s if d == 0 else u < s
        earlier = u < s if d == 0 else u > s
        put(f"nF{d}", -(later & block).astype(np.float32))
        put(f"eF{d}", (later & ~block).astype(np.float32))
        put(f"nP{d}", -(earlier & block).astype(np.float32))
        put(f"sF{d}", later.astype(np.float32))
        put(f"iF{d}", (later | (u == s)).astype(np.float32))
    return out


class Region:

    def __init__(self, tensor, start, end):
        self.tensor, self.at, self.end = tensor, start, end

    def take(self, *shape):
        n = int(np.prod(shape))
        v = self.tensor[:, self.at:self.at + n]
        self.at += n
        assert self.at <= self.end, (self.at, self.end)
        if len(shape) == 2:
            v = v.rearrange("p (a b) -> p a b", b=shape[1])
        if len(shape) == 3:
            v = v.rearrange("p (a b c) -> p a b c", b=shape[1], c=shape[2])
        return v


@contextmanager
def phase_semaphores(nc):
    given = []

    def sem(name):
        given.append(nc.alloc_semaphore(name))
        return given[-1]

    yield sem
    nc.clear_and_free_semaphores(given)
    nc.all_engine_barrier()


class Steps:

    def __init__(self, eng, own):
        self.eng, self.own, self.count = eng, own, {}

    def __call__(self, ins, sem=None):
        sem = self.own if sem is None else sem
        self.count[sem.name] = self.count.get(sem.name, 0) + 1
        ins.then_inc(sem, 1)
        self.eng.wait_ge(sem, self.count[sem.name])


ARENA = 41 * 1024 + 768


def build(nc, a):
    with ExitStack() as ctx:
        sb = lambda n, s, dt=F32: ctx.enter_context(nc.sbuf_tensor(n, s, dt))
        cst = sb("cst", [P, NCONST])
        par = sb("par", [P, NPAR, KT])
        xl = sb("xl", [P, TT, D])
        MT = sb("MT", [P, KT, NTOK])
        modT = sb("modT", [P, 48, 2])
        npost = sb("npost", [P, 3, KT])
        PS = ctx.enter_context(nc.psum_tensor("PS", [P, 8, 512], F32))
        zw_loaded = [ctx.enter_context(nc.semaphore(f"zw_loaded{s}")) for s in range(NSLOT)]
        lu_loaded = ctx.enter_context(nc.semaphore("lu_loaded"))
        wout_loaded = ctx.enter_context(nc.semaphore("wout_loaded"))
        k = lambda n: cst[:, CONST[n][0]:CONST[n][0] + CONST[n][1]]
        f = sb("f", [P, TT, D])
        pp, gg = sb("pp", [P, TT, 2 * NE + 2]), sb("gg", [P, TT, 2 * NE + 2])
        rowv = sb("rowv", [P, 1, D])
        count = sb("count", [P, 1], I32)
        shared = dict(f=f, pp=pp, gg=gg, rowv=rowv, count=count, nc=nc, a=a, k=k, par=par, xl=xl, MT=MT[:, :, :],
                      modT=modT, npost=npost, PS=PS, cst=cst,
                      zw_loaded=zw_loaded, lu_loaded=lu_loaded, wout_loaded=wout_loaded)
        with nc.sbuf_tensor("arena", [P, ARENA], F32) as arena:
            r = Region(arena, 0, ARENA)
            first = dict(arena=arena, zw=r.take(NSLOT, KT, P), hT=r.take(KT, T), free=r.at)
            adaln(**shared, **first)
            mixing(**shared, **first)
            project(**shared, **first)
        experts(**shared)


def adaln(nc, a, k, par, xl, modT, npost, arena, PS, zw, hT, free, cst, zw_loaded, **_):
    with ExitStack() as ctx:
        sem = ctx.enter_context(phase_semaphores(nc))
        r = Region(arena, free, ARENA)
        w = r.take(KT, 2048)
        xc = r.take(TT, D)
        xn = r.take(2, D)
        sq = r.take(D)
        cT = r.take(KT, 2)
        csil = r.take(KT, 2)
        rows = r.take(2048)
        stat = r.take(4, 3)
        bada = r.take(48)
        tmp = r.take(KT, 2)
        scale = r.take(KT, 2)
        consts_in, small_in, x_in = sem("consts_in"), sem("small_in"), [sem(f"x_in{i}") for i in range(4)]
        ada_in = [sem(f"ada_in{i}") for i in range(KT)]
        ada_used = [sem(f"ada_used{i}") for i in range(KT)]
        silu_ready, rows_ev, cols_mm, cols_ev = (sem(n) for n in ("silu_ready", "rows_ev", "cols_mm", "cols_ev"))
        ss_ready, ms_ready, rms_ready, xn_ready, xt_mm, xt_ev = (sem(n) for n in ("ss_ready", "ms_ready", "rms_ready", "xn_ready", "xt_mm", "xt_ev"))
        sig_ready, turning, vec, act_seq = sem("sig_ready"), sem("turning"), sem("vec_steps"), sem("act_steps")
        block = ctx.enter_context(nc.Block())

        def tile_of(i):
            return xc[:, i, :] if i < TT else xl[:, i - TT, :]

        @block.sync
        def _(sp):
            sp.dma_start(cst[:, :], a["consts"]).then_inc(consts_in, 16)
            for i in range(4):
                src = a["ctx"] if i < TT else a["x"]
                t0 = (i % TT) * P
                sp.dma_start(tile_of(i), src[t0:t0 + P, :]).then_inc(x_in[i], 16)
            with sp.Fori(0, 3) as g:
                for kt in range(KT):
                    sp.wait_ge(ada_used[kt], g + 1)
                    sp.dma_start(w[:, kt, :], a["w_ada"][kt * P:(kt + 1) * P, bass.ds(g * 2048, 2048)]).then_inc(ada_in[kt], 16)
            for s in range(NSLOT):
                b = s if s < 3 else 3 + s
                sp.dma_start(zw[:, s, :, :], a["w_blk"][b]).then_inc(zw_loaded[s], 16)

        @block.gpsimd
        def _(pool):
            pool.dma_start(cT, a["cT"]).then_inc(small_in, 16)
            pool.dma_start(par[:, 0:NHOST, :], a["par"]).then_inc(small_in, 16)
            pool.dma_start(bada, a["b_ada"]).then_inc(small_in, 16)
            pool.dma_start(npost[:, :, :], a["npost"]).then_inc(small_in, 16)

        @block.scalar
        def _(act):
            step = Steps(act, act_seq)
            act.wait_ge(small_in, 64)
            step(nc.scalar.activation(tmp, cT, ACT.Sigmoid), sig_ready)
            for i in range(4):
                act.wait_ge(x_in[i], 16)
                step(nc.scalar.activation(sq, tile_of(i), ACT.Square, accum_out=stat[:, i, 0:1]), ss_ready)
            for i in range(4):
                act.wait_ge(ms_ready, 1 + i)
                step(nc.scalar.activation(stat[:, i, 2:3], stat[:, i, 1:2], ACT.Sqrt), rms_ready)
            act.sem_inc(rows_ev, 1)
            with act.Fori(0, 3) as g:
                act.wait_ge(ada_used[KT - 1], g + 2)
                act.wait_ge(cols_mm, g + 1)
                for n in range(4):
                    ins = nc.scalar.activation(rows[0:2, n * 512:(n + 1) * 512], PS[0:2, n, :], ACT.Copy)
                ins.then_inc(rows_ev, 1)

        @block.tensor
        def _(pe):
            pe.wait_ge(consts_in, 16)
            for i in range(4):
                pe.wait_ge(xn_ready, i + 1)
                for kt in range(KT):
                    if kt % 4 == 0 and i > 0:
                        pe.wait_ge(xt_ev, 2 * (i - 1) + kt // 4 + 1)
                    ins = nc.tensor.transpose(PS[:, 4 + kt // 4, (kt % 4) * P:(kt % 4 + 1) * P],
                                              xn[:, i % 2, kt * P:(kt + 1) * P], k("ident"))
                    if kt % 4 == 3:
                        ins.then_inc(xt_mm, 1)
            pe.wait_ge(silu_ready, 1)
            pe.sem_inc(cols_mm, 1)
            for kt in range(KT):
                pe.sem_inc(ada_used[kt], 1)
            with pe.Fori(0, 3) as g:
                pe.wait_ge(rows_ev, g + 1)
                for kt in range(KT):
                    pe.wait_ge(ada_in[kt], g * 16 + 16)
                    pe.wait_ge(silu_ready, 1)
                    for n in range(4):
                        ins = nc.tensor.matmul(PS[0:2, n, :], csil[:, kt, :], w[:, kt, n * 512:(n + 1) * 512],
                                               start=kt == 0, stop=kt == KT - 1)
                    ins.then_inc(ada_used[kt], 1)
                pe.wait_ge(rows_ev, g + 2)
                pe.wait_ge(cols_ev, g + 1)
                pe.sem_inc(turning, 1)
                for m in range(16):
                    ins = nc.tensor.transpose(PS[:, 6, 2 * m:2 * m + 2], rows[0:2, m * P:(m + 1) * P], k("ident")[0:2, 0:2])
                ins.then_inc(cols_mm, 1)

        @block.vector
        def _(dve):
            step = Steps(dve, vec)
            dve.wait_ge(small_in, 64)
            dve.wait_ge(consts_in, 16)
            dve.wait_ge(sig_ready, 1)
            nc.vector.tensor_tensor(csil, tmp, cT, ALU.mult).then_inc(silu_ready, 1)
            pp = lambda n: par[:, PAR[n], :]
            for n in ("w0_0", "w0_1", "a0_0", "a0_1"):
                nc.vector.tensor_scalar(pp("h" + n), pp(n), 0.5, None, ALU.mult)
            nc.vector.tensor_scalar(pp("hka"), pp("k_a"), 0.5, None, ALU.mult)
            nc.vector.tensor_scalar(pp("omka"), pp("k_a"), -0.5, 1.0, ALU.mult, ALU.add)
            step(nc.vector.tensor_scalar(pp("hrk"), pp("r_k"), 0.5, None, ALU.mult))
            for t in "kvr":
                mixing_weights(nc, step, k, lambda n: pp(f"{n}_{t}"), pp(f"mu_{t}"))
            for i in range(4):
                dve.wait_ge(ss_ready, i + 1)
            for i in range(4):
                ins = nc.vector.tensor_scalar(stat[:, i, 1:2], stat[:, i, 0:1], 1.0 / D, EPS, ALU.mult, ALU.add)
                ins.then_inc(ms_ready, 1)
            for i in range(4):
                dve.wait_ge(rms_ready, i + 1)
                step(nc.vector.reciprocal(stat[:, i, 1:2], stat[:, i, 2:3]))
                if i >= 2:
                    dve.wait_ge(xt_mm, 2 * (i - 1))
                nc.vector.tensor_scalar(xn[:, i % 2, :], tile_of(i), stat[:, i, 1:2], None, ALU.mult).then_inc(xn_ready, 1)
                for half in range(2):
                    dve.wait_ge(xt_mm, 2 * i + half + 1)
                    src = PS[:, 4 + half, :].rearrange("p (q t) -> p q t", t=P)
                    nc.vector.tensor_copy(hT[:, 4 * half:4 * half + 4, i * P:(i + 1) * P], src).then_inc(xt_ev, 1)
            dve.sem_inc(cols_ev, 1)
            with dve.Fori(0, 3) as g:
                dve.wait_ge(consts_in, 16)
                dve.wait_ge(cols_mm, g + 2)
                src = PS[:, 6, 0:32].rearrange("p (m s) -> p m s", s=2)
                nc.vector.tensor_copy(modT[:, bass.ds(g * 16, 16), :], src).then_inc(cols_ev, 1)
            dve.wait_ge(cols_ev, 4)
            step(nc.vector.tensor_tensor(modT[:, :, :], modT[:, :, :], bada.unsqueeze(2).broadcast_to([P, 48, 2]), ALU.add))
            for s in range(2):
                nc.vector.tensor_scalar(scale[:, :, s], modT[:, KT:2 * KT, s], 1.0, None, ALU.add)
            step(nc.vector.tensor_copy(stat[:, 0, 0:1], stat[:, 0, 1:2]))
            for s in range(2):
                ins = nc.vector.tensor_tensor(scale[:, :, s], scale[:, :, s], pp("npm"), ALU.mult)
            step(ins)
            dve.wait_ge(xt_ev, 8)
            for kt in range(KT):
                for s, t0 in ((1, 0), (0, NTOK)):
                    v = hT[:, kt, t0:t0 + NTOK]
                    ins = nc.vector.tensor_scalar(v, v, scale[:, kt, s:s + 1], modT[:, kt, s:s + 1], ALU.mult, ALU.add)
            step(ins)


def mixing_weights(nc, step, k, out, mu):
    for q in range(4):
        nc.vector.tensor_scalar(out(f"q{q}"), mu, k("cls")[:, q:q + 1], None, ALU.mult)
    step(nc.vector.tensor_scalar(out("om"), mu, -1.0, 1.0, ALU.mult, ALU.add))
    nc.vector.tensor_tensor(out("prev"), out("q0"), out("q2"), ALU.add)
    step(nc.vector.tensor_tensor(out("next"), out("q1"), out("q3"), ALU.add))


def qshift(nc, step, z, out, col, done, ctx_tokens=True):
    t0 = NTOK if ctx_tokens else 0
    add = lambda o, i, m, s=None: step(nc.vector.scalar_tensor_tensor(
        out=o, in0=i, scalar=col(m), in1=o, op0=ALU.mult, op1=ALU.add), s)
    if ctx_tokens:
        add(out[:, 1:NTOK], z[:, 0:NTOK - 1], "prev")
        add(out[:, 0:NTOK - 1], z[:, 1:NTOK], "next")
    rows = lambda v: v[:, t0:t0 + NTOK].rearrange("p (r w) -> p r w", w=GRID_W)
    o, i = rows(out), rows(z)
    add(o[:, :, 1:GRID_W], i[:, :, 0:GRID_W - 1], "q0")
    add(o[:, :, 0:GRID_W - 1], i[:, :, 1:GRID_W], "q1")
    add(out[:, t0 + GRID_W:t0 + NTOK], z[:, t0:t0 + NTOK - GRID_W], "q2")
    add(out[:, t0:t0 + NTOK - GRID_W], z[:, t0 + GRID_W:t0 + NTOK], "q3", done)


def mixing(nc, a, k, par, MT, arena, PS, zw, hT, free, zw_loaded, lu_loaded, wout_loaded, **_):
    with ExitStack() as ctx:
        sem = ctx.enter_context(phase_semaphores(nc))
        r = Region(arena, free, ARENA)
        lu = r.take(3, P)
        mu_sh = r.take(3)
        mx = {m: r.take(3) for m in MIX}
        twT, laT, sgT = r.take(T), r.take(T), r.take(NTOK)
        pj = r.take(NPAR)
        k_sh, v_sh, r_sh = r.take(T), r.take(T), r.take(NTOK)
        TW, TA, CUM, E1, E2 = ([r.take(T) for d in (0, 1)] for _ in range(5))
        AL, BE, KA = ([r.take(NC, C) for d in (0, 1)] for _ in range(3))
        RH = [r.take(NL, C) for d in (0, 1)]
        KK, KD = r.take(T), [r.take(T) for d in (0, 1)]
        PC = [r.take(NC) for d in (0, 1)]
        AT, BT, KTK = ([r.take(NC, C) for d in (0, 1)] for _ in range(3))
        VT = r.take(NC, C)
        NF, NP, EF, KF = ([r.take(NC, C) for d in (0, 1)] for _ in range(4))
        RB, RK = ([r.take(NL, C) for d in (0, 1)] for _ in range(2))
        YY = [r.take(NC, C) for d in (0, 1)]
        SS = [r.take(NC - 1, C) for d in (0, 1)]
        SP_ = [r.take(C) for d in (0, 1)]
        GAT, ZB, ZX = r.take(T), r.take(T), r.take(T)
        ys, yc, yq, bo, cu, cv, ct = (r.take(NTOK) for _ in range(7))
        chunks = lambda v: v.rearrange("p (c t) -> p c t", t=C)
        Q0P, Q0F = [chunks(v) for v in TW], [chunks(v) for v in TA]
        Q1P, Q1F = [chunks(v) for v in CUM], [chunks(v) for v in E2]
        WT, X, U0, UN = NF, NP, AL, KA
        TP, ET = Q0P, Q0F

        iter_done, iter_go = sem("iter_done"), sem("iter_go")
        shared_mm, shared_om, shared_dn, lora_ready = (sem(n) for n in ("shared_mm", "shared_om", "shared_dn", "lora_ready"))
        mu_in, seq0 = sem("mu_in"), sem("dve_prelude")
        first = sem("loop_sems_begin")
        names = ["pj_ready", "z_mm", "om_ev", "k_dn", "v_dn", "r_dn", "lora_mm", "tw_ev", "ta_ev", "sq_ev", "ssq_mm",
                 "ssq_dn", "nrm_ev", "cum_dn", "e_ev", "gate_mm", "r2_ev", "feat_dn", "vt_mm", "vt_ev", "bon_dn",
                 "y_mm", "y_ev", "mean_mm", "yc_dn", "yq_ev", "var_mm", "var_dn", "std_ev", "bonus_mm", "pool_seq",
                 "conv_dn", "all_passed", "dve_seq", "act_seq", "y1_dn"]
        names += [f"{n}{d}" for d in (0, 1) for n in ("u_mm", "un_ev", "s_mm", "s_ev")]
        JOBS = ["G1", "G2", "G3", "G4", "AT", "N2P", "N2F", "BT", "KT", "Y2", "N4P", "N4F", "Y4", "N8P", "N8F",
                "Y8", "N16P", "Y16", "TP", "X", "ET", "Y64", "WT", "U0"]
        names += [f"{j}_{w}" for j in JOBS for w in ("mm", "ev")]
        S = {n: sem(n) for n in names}
        loop_sems = range(first.num + 1, first.num + 1 + len(names))
        assert [S[n].num for n in names] == list(loop_sems)
        order = [list(range(NC)), list(range(NL - 1, -1, -1)) + list(range(NC - 1, NL - 1, -1))]
        H = [slice(C * h, C * h + C) for h in (0, 1)]
        bank = {"c": (0, 1), "s": (2, 7), "a": (3, 5), "b": (4, 6)}
        bk = lambda n, d: PS[:, bank[n][d], :].rearrange("p (c t) -> p c t", t=C)
        k2 = lambda n: k(n).unsqueeze(1).broadcast_to([P, NC, C])
        c_ = lambda n: pj[:, PAR[n]:PAR[n] + 1]

        block = ctx.enter_context(nc.Block())

        @block.sync
        def _(sp):
            sp.dma_start(mu_sh, a["mu_sh"]).then_inc(mu_in, 16)
            sp.dma_start(lu, a["lora_up"][0]).then_inc(lu_loaded, 16)
            for s in range(3):
                sp.wait_ge(shared_mm, s + 1)
                sp.dma_start(zw[:, s, :, :], a["w_blk"][3 + s]).then_inc(zw_loaded[s], 16)

            def body(j, more):
                for s in range(NSLOT):
                    sp.wait_ge(S["z_mm"], s + 1)
                    if more:
                        sp.dma_start(zw[:, s, :, :], a["w_blk"][bass.ds(j * NSLOT + (3 + NSLOT + s), 1)].rearrange("o p k c -> p (o k) c")).then_inc(zw_loaded[s], 16)
                sp.wait_ge(S["gate_mm"], 1)
                if more:
                    sp.dma_start(lu, a["lora_up"][bass.ds(j + 1, 1)].rearrange("o p k c -> p (o k) c")).then_inc(lu_loaded, 16)
                sp.sem_inc(iter_done, 1)
                sp.wait_ge(shared_mm, 3)
                sp.wait_ge(iter_go, j + 1)

            with sp.Fori(0, KT - 1) as j:
                body(j, True)
            body(KT - 1, False)
            sp.dma_start(zw.rearrange("p s k c -> p (s k c)").rearrange("p (q n) -> p q n", n=D),
                         a["w_out"].rearrange("(q p) n -> p q n", p=P)).then_inc(wout_loaded, 16)

        @block.gpsimd
        def _(pool):
            with pool.Fori(0, KT) as j:
                step = Steps(pool, S["pool_seq"])
                pool.wait_ge(S["pj_ready"], 1)
                pool.wait_ge(S["r2_ev"], 3)
                tt, ts = nc.gpsimd.tensor_tensor, nc.gpsimd.tensor_scalar
                step(tt(cu, ZB[:, NTOK:T], ZX[:, 0:NTOK], ALU.mult))
                step(ts(cv, cu, c_("cw1"), 0.0, ALU.mult, ALU.add))
                step(ts(ct[:, 0:NTOK - 1], cu[:, 0:NTOK - 1], c_("cw0"), 0.0, ALU.mult, ALU.add))
                step(tt(cv[:, 1:NTOK], cv[:, 1:NTOK], ct[:, 0:NTOK - 1], ALU.add))
                step(ts(ct[:, 1:NTOK], cu[:, 1:NTOK], c_("cw2"), 0.0, ALU.mult, ALU.add))
                step(tt(cv[:, 0:NTOK - 1], cv[:, 0:NTOK - 1], ct[:, 1:NTOK], ALU.add))
                step(tt(cv, cv, ZB[:, 0:NTOK], ALU.mult))
                step(ts(GAT, GAT, 0.5, 0.5, ALU.mult, ALU.add))
                step(tt(cv, cv, GAT[:, NTOK:T], ALU.mult), S["conv_dn"])
                pool.wait_ge(iter_done, j * 4 + 4)
                pool.sem_inc(S["all_passed"], 1)
                pool.wait_ge(S["all_passed"], 1)
                pool.sem_clear(loop_sems)
                pool.sem_inc(iter_go, 1)

        @block.scalar
        def _(act):
            A = nc.scalar.activation
            act.wait_ge(seq0, 1)
            for i, o in enumerate((twT, laT, sgT)):
                n = NTOK if i == 2 else T
                act.wait_ge(shared_mm, i + 1)
                A(o, PS[:, i, 0:n], ACT.Copy, scale=mx["om"][:, i:i + 1]).then_inc(shared_om, 1)
            act.wait_ge(shared_dn, 1)
            A(twT, twT, ACT.Tanh).then_inc(lora_ready, 1)
            act.wait_ge(shared_dn, 3)
            A(sgT, sgT, ACT.Sigmoid).then_inc(lora_ready, 1)
            with act.Fori(0, KT) as j:
                step = Steps(act, S["act_seq"])
                act.wait_ge(S["pj_ready"], 1)
                for i, (o, n, t) in enumerate(((k_sh, T, "k"), (v_sh, T, "v"), (r_sh, NTOK, "r"))):
                    act.wait_ge(S["z_mm"], i + 1)
                    step(A(o, PS[:, i, 0:n], ACT.Copy, scale=c_(f"om_{t}")), S["om_ev"])
                for d in (0, 1):
                    act.wait_ge(S["lora_mm"], d + 1)
                    step(A(TW[d], PS[:, 3 + d, :], ACT.Tanh, scale=0.5, bias=c_(f"hw0_{d}")), S["tw_ev"])
                for d in (0, 1):
                    act.wait_ge(S["lora_mm"], d + 3)
                    step(A(TA[d], PS[:, 5 + d, :], ACT.Tanh, scale=0.5, bias=c_(f"ha0_{d}")), S["ta_ev"])
                act.wait_ge(S["k_dn"], 1)
                step(A(KK, k_sh, ACT.Square, scale=c_("k_k")), S["sq_ev"])
                act.wait_ge(S["ssq_dn"], 1)
                step(A(KK, KK, ACT.Sqrt), S["nrm_ev"])
                for d in (0, 1):
                    act.wait_ge(S["cum_dn"], d + 1)
                    step(A(E1[d], CUM[d], ACT.Exp), S["e_ev"])
                    step(A(E2[d], CUM[d], ACT.Exp, scale=-1.0), S["e_ev"])
                act.wait_ge(S["z_mm"], 5)
                step(A(GAT, PS[:, 0, :], ACT.Tanh, scale=0.5), S["r2_ev"])
                act.wait_ge(S["z_mm"], 7)
                step(A(ZB, PS[:, 1, :], ACT.Copy), S["r2_ev"])
                act.wait_ge(S["gate_mm"], 1)
                step(A(ZX, PS[:, 2, :], ACT.Copy), S["r2_ev"])

                def halves(job, out, d, b):
                    act.wait_ge(S[f"{job}_mm"], d + 1)
                    src = PS[:, b, :].rearrange("p (q n) -> p q n", n=P)
                    to = out.rearrange("p (q e) c -> p q e c", e=2)
                    for h in (0, 1):
                        for e in (0, 1):
                            ins = A(to[H[h], :, e, :], src[H[e], :, H[h]], ACT.Copy)
                            if (h, e) != (1, 1):
                                step(ins)
                    step(ins, S[f"{job}_ev"])

                def copy(job, out, d, b):
                    act.wait_ge(S[f"{job}_mm"], d + 1)
                    step(A(out[d], bk(b, d), ACT.Copy), S[f"{job}_ev"])

                halves("vt", VT, 0, bank["a"][0])
                for d in (0, 1):
                    halves("AT", AT[d], d, bank["a"][d])
                for d in (0, 1):
                    copy("N2P", Q0P, d, "c")
                for d in (0, 1):
                    copy("N2F", Q0F, d, "s")
                for job, out in (("BT", BT), ("KT", KTK)):
                    for d in (0, 1):
                        halves(job, out[d], d, bank["a"][d])
                for job, out, b in (("N4P", Q1P, "b"), ("N4F", Q1F, "c"), ("N8P", Q0P, "a"), ("N8F", Q0F, "b"),
                                    ("N16P", Q1P, "s"), ("TP", TP, "b"), ("X", X, "c"), ("ET", ET, "a"),
                                    ("WT", WT, "b"), ("U0", U0, "c")):
                    for d in (0, 1):
                        copy(job, out, d, b)
                act.wait_ge(S["y_mm"], 1)
                step(A(ys, PS[:, 0, 0:NTOK], ACT.Copy), S["y_ev"])
                act.wait_ge(S["yc_dn"], 1)
                step(A(yq, yc, ACT.Square), S["yq_ev"])
                act.wait_ge(S["var_dn"], 1)
                step(A(yq, yq, ACT.Sqrt), S["std_ev"])
                act.sem_inc(iter_done, 1)
                act.wait_ge(iter_go, j + 1)

        @block.tensor
        def _(pe):
            mm = nc.tensor.matmul

            def zblock(slot, out, t0, N, signal):
                for kt in range(KT):
                    ins = mm(out, zw[:, slot, kt, :], hT[:, kt, t0:t0 + N], start=kt == 0, stop=kt == KT - 1)
                ins.then_inc(signal, 1)

            for s, (t0, N) in enumerate(((0, T), (0, T), (NTOK, NTOK))):
                pe.wait_ge(zw_loaded[s], 16)
                zblock(s, PS[:, s, 0:N], t0, N, shared_mm)
            pe.wait_ge(lora_ready, 2)
            pe.wait_ge(shared_dn, 3)
            with pe.Fori(0, KT) as j:
                for s, (t0, N) in enumerate(((0, T), (0, T), (NTOK, NTOK))):
                    pe.wait_ge(zw_loaded[s], j * 16 + 32)
                    zblock(s, PS[:, s, 0:N], t0, N, S["z_mm"])
                pe.wait_ge(lu_loaded, j * 16 + 16)
                pe.wait_ge(shared_dn, 3)
                for i, src in enumerate((twT, laT)):
                    for d in (0, 1):
                        mm(PS[:, 3 + 2 * i + d, :], lu[H[d], i, :], src[H[d], :], start=True, stop=True).then_inc(S["lora_mm"], 1)
                pe.wait_ge(S["k_dn"], 1)
                for i, s in enumerate((3, 4)):
                    pe.wait_ge(zw_loaded[s], j * 16 + 16)
                    zblock(s, PS[:, 0, i * NTOK:(i + 1) * NTOK], NTOK, NTOK, S["z_mm"])
                pe.wait_ge(S["sq_ev"], 1)
                mm(PS[:, 7, :], k("heads"), KK, start=True, stop=True).then_inc(S["ssq_mm"], 1)
                pe.wait_ge(S["v_dn"], 1)
                for i, s in enumerate((5, 6)):
                    pe.wait_ge(zw_loaded[s], j * 16 + 16)
                    zblock(s, PS[:, 1, i * NTOK:(i + 1) * NTOK], NTOK, NTOK, S["z_mm"])
                pe.wait_ge(S["r_dn"], 1)
                pe.wait_ge(zw_loaded[7], j * 16 + 16)
                zblock(7, PS[:, 2, 0:NTOK], NTOK, NTOK, S["z_mm"])
                mm(PS[:, 2, NTOK:T], lu[:, 2, :], sgT, start=True, stop=True).then_inc(S["gate_mm"], 1)

                def waits(d, *products):
                    for n in products:
                        pe.wait_ge(S[n], d + 1)

                def unit(job, b, d, lhsT, rhs):
                    out = bk(b, d)
                    for c in range(NC):
                        for h in (0, 1):
                            ins = mm(out[H[h], c, :], lhsT[H[h], c, :], rhs[H[h], c, :], start=True, stop=True)
                    ins.then_inc(S[f"{job}_mm"], 1)

                def turn(job, b, src):
                    for q in range(NC // 2):
                        ins = nc.tensor.transpose(PS[:, b, q * P:(q + 1) * P], src[:, 2 * q:2 * q + 2, :], k("ident"))
                    ins.then_inc(S[f"{job}_mm"], 1)

                pe.wait_ge(S["v_dn"], 1)
                pe.wait_ge(S["tw_ev"], 2)
                turn("vt", bank["a"][0], chunks(v_sh))
                pe.wait_ge(S["ta_ev"], 2)
                pe.wait_ge(S["r2_ev"], 3)
                pe.wait_ge(S["ssq_dn"], 1)
                for d in (0, 1):
                    waits(d, "feat_dn")
                    unit("G1", "c", d, BE[d], AL[d])
                for d in (0, 1):
                    if d == 0:
                        pe.wait_ge(S["vt_ev"], 1)
                    unit("G2", "a", d, AL[d], BE[d])
                for d in (0, 1):
                    unit("G3", "b", d, KA[d], AL[d])
                for d in (0, 1):
                    out = bk("s", d)
                    for c in range(NL):
                        for h in (0, 1):
                            mm(out[H[h], c, :], BE[d][H[h], NL + c, :], RH[d][H[h], c, :], start=True, stop=True)
                            ins = mm(out[H[h], NL + c, :], KA[d][H[h], NL + c, :], RH[d][H[h], c, :], start=True, stop=True)
                    ins.then_inc(S["G4_mm"], 1)
                for d in (0, 1):
                    waits(d, "G2_ev", "G3_ev")
                    turn("AT", bank["a"][d], AL[d])
                for d in (0, 1):
                    waits(d, "G1_ev")
                    unit("N2P", "c", d, NF[d], NP[d])
                for d in (0, 1):
                    waits(d, "G4_ev")
                    unit("N2F", "s", d, NP[d], NF[d])
                for job, src, before in (("BT", BE, "AT_ev"), ("KT", KA, "BT_ev")):
                    for d in (0, 1):
                        waits(d, before)
                        turn(job, bank["a"][d], src[d])
                for job, b, lhsT, rhs, need in (
                    ("Y2", "a", Q0P, YY, ("N2P_ev", "KT_ev", "y1_dn")),
                    ("N4P", "b", Q0F, Q0P, ("N2F_ev",)),
                    ("N4F", "c", Q0P, Q0F, ()),
                    ("Y4", "s", Q1P, YY, ("N4P_ev", "Y2_ev")),
                    ("N8P", "a", Q1F, Q1P, ("N4F_ev",)),
                    ("N8F", "b", Q1P, Q1F, ()),
                    ("Y8", "c", Q0P, YY, ("N8P_ev", "Y4_ev")),
                    ("N16P", "s", Q0F, Q0P, ("N8F_ev",)),
                    ("Y16", "a", Q1P, YY, ("N16P_ev", "Y8_ev")),
                    ("TP", "b", YY, None, ("Y16_ev",)),
                    ("X", "c", KF, [VT, VT], ()),
                    ("ET", "a", EF, TP, ("TP_ev",)),
                    ("Y64", "s", ET, YY, ("ET_ev",)),
                    ("WT", "b", AT, YY, ("Y64_ev",)),
                    ("U0", "c", YY, X, ("X_ev",)),
                ):
                    for d in (0, 1):
                        waits(d, *need)
                        if rhs is None:
                            out = bk(b, d)
                            for c in range(NC):
                                for h in (0, 1):
                                    ins = mm(out[H[h], c, :], lhsT[d][H[h], c, :], k("ident")[H[h], H[h]], start=True, stop=True)
                            ins.then_inc(S[f"{job}_mm"], 1)
                        else:
                            unit(job, b, d, lhsT[d], rhs[d])
                for d in (0, 1):
                    waits(d, "WT_ev", "U0_ev", "ET_ev")
                for i in range(NC):
                    for d in (0, 1):
                        c = order[d][i]
                        if i > 0:
                            pe.wait_ge(S[f"s_ev{d}"], i)
                            for h in (0, 1):
                                ins = mm(PS[H[h], bank["a"][d], 0:C], WT[d][H[h], c, :], SS[d][H[h], i - 1, :], start=True, stop=True)
                            ins.then_inc(S[f"u_mm{d}"], 1)
                    if i == NC - 1:
                        break
                    for d in (0, 1):
                        c = order[d][i]
                        pe.wait_ge(S[f"un_ev{d}"], i + 1)
                        for h in (0, 1):
                            out = PS[H[h], bank["b"][d], 0:C]
                            mm(out, BT[d][H[h], c, :], UN[d][H[h], c, :], start=True, stop=False)
                            ins = mm(out, KTK[d][H[h], c, :], VT[H[h], c, :], start=False, stop=True)
                        ins.then_inc(S[f"s_mm{d}"], 1)
                pe.wait_ge(S["bon_dn"], 1)
                mm(PS[:, 7, 0:NTOK], k("heads"), bo, start=True, stop=True).then_inc(S["bonus_mm"], 1)
                for d in (0, 1):
                    pe.wait_ge(S[f"un_ev{d}"], NC)
                for c in range(NL):
                    for h in (0, 1):
                        out = PS[H[h], 0, c * C:(c + 1) * C]
                        for d in (0, 1):
                            i = order[d].index(NL + c)
                            mm(out, SS[d][H[h], i - 1, :], RH[d][H[h], c, :], start=d == 0, stop=False)
                            mm(out, UN[d][H[h], NL + c, :], RB[d][H[h], c, :], start=False, stop=False)
                            ins = mm(out, VT[H[h], NL + c, :], RK[d][H[h], c, :], start=False, stop=d == 1)
                ins.then_inc(S["y_mm"], 1)
                pe.wait_ge(S["y_ev"], 1)
                mm(PS[:, 1, 0:NTOK], k("headmean"), ys, start=True, stop=True).then_inc(S["mean_mm"], 1)
                pe.wait_ge(S["yq_ev"], 1)
                mm(PS[:, 2, 0:NTOK], k("headmean"), yq, start=True, stop=True).then_inc(S["var_mm"], 1)
                pe.sem_inc(iter_done, 1)
                pe.wait_ge(iter_go, j + 1)

        @block.vector
        def _(dve):
            tt, ts, stt = nc.vector.tensor_tensor, nc.vector.tensor_scalar, nc.vector.scalar_tensor_tensor
            step = Steps(dve, seq0)
            dve.wait_ge(mu_in, 16)
            for q in range(4):
                ts(mx[f"q{q}"], mu_sh, k("cls")[:, q:q + 1], None, ALU.mult)
            step(ts(mx["om"], mu_sh, -1.0, 1.0, ALU.mult, ALU.add))
            tt(mx["prev"], mx["q0"], mx["q2"], ALU.add)
            step(tt(mx["next"], mx["q1"], mx["q3"], ALU.add))
            for i, o in enumerate((twT, laT, sgT)):
                n = NTOK if i == 2 else T
                dve.wait_ge(shared_om, i + 1)
                qshift(nc, step, PS[:, i, 0:n], o, lambda m: mx[m][:, i:i + 1], shared_dn, i < 2)
            dve.wait_ge(lora_ready, 2)
            with dve.Fori(0, KT) as j:
                step = Steps(dve, S["dve_seq"])
                step(nc.vector.tensor_copy(pj, par[:, :, bass.ds(j, 1)].rearrange("p n o -> p (n o)")), S["pj_ready"])
                dve.wait_ge(S["om_ev"], 1)
                qshift(nc, step, PS[:, 0, :], k_sh, lambda m: c_(m + "_k"), S["k_dn"])
                for d in (0, 1):
                    dve.wait_ge(S["tw_ev"], d + 1)
                    step(ts(TW[d], TW[d], DECAY_C, DECAY_C, ALU.mult, ALU.add))
                    o, w, m = CUM[d], TW[d], k(f"scan{d}")
                    if d == 1:
                        o, w, m = o[:, ::-1], w[:, ::-1], m[:, ::-1]
                    step(nc.vector.tensor_tensor_scan(o, m, w, 0.0, ALU.mult, ALU.add), S["cum_dn"])
                dve.wait_ge(S["om_ev"], 2)
                qshift(nc, step, PS[:, 1, :], v_sh, lambda m: c_(m + "_v"), S["v_dn"])
                dve.wait_ge(S["om_ev"], 3)
                qshift(nc, step, PS[:, 2, 0:NTOK], r_sh, lambda m: c_(m + "_r"), S["r_dn"], False)
                dve.wait_ge(S["ssq_mm"], 1)
                step(ts(KK, PS[:, 7, :], 1e-24, None, ALU.max), S["ssq_dn"])
                for d in (0, 1):
                    dve.wait_ge(S["ta_ev"], d + 1)
                    step(ts(KD[d], TA[d], c_("hka"), c_("omka"), ALU.mult, ALU.add))
                    step(tt(KD[d], KD[d], k_sh, ALU.mult))
                    step(ts(TA[d], TA[d], 0.5, 0.5, ALU.mult, ALU.add))
                dve.wait_ge(S["nrm_ev"], 1)
                step(nc.vector.reciprocal(KK, KK))
                step(stt(out=KK, in0=k_sh, scalar=c_("k_k"), in1=KK, op0=ALU.mult, op1=ALU.mult))
                for d in (0, 1):
                    step(tt(TA[d], KK, TA[d], ALU.mult))
                    dve.wait_ge(S["e_ev"], 2 * d + 2)
                    e1, kk = chunks(E1[d]), chunks(KK)
                    step(tt(BE[d], chunks(TA[d]), chunks(E2[d]), ALU.mult))
                    step(tt(KA[d], chunks(KD[d]), chunks(E2[d]), ALU.mult))
                    ahead, behind = (slice(1, C), slice(0, C - 1)) if d == 0 else (slice(0, C - 1), slice(1, C))
                    edge, last = (0, C - 1) if d == 0 else (C - 1, 0)
                    step(tt(AL[d][:, :, ahead], kk[:, :, ahead], e1[:, :, behind], ALU.mult))
                    step(nc.vector.tensor_copy(AL[d][:, :, edge:edge + 1], kk[:, :, edge:edge + 1]))
                    step(tt(RH[d], chunks(r_sh), e1[:, NL:NC, :], ALU.mult))
                    step(nc.vector.tensor_copy(PC[d].unsqueeze(2), e1[:, :, last:last + 1]), S["feat_dn"])
                for d in (0, 1):
                    dve.wait_ge(S["G1_mm"], d + 1)
                    step(tt(NF[d], bk("c", d), k2(f"nF{d}"), ALU.mult))
                    step(tt(EF[d], bk("c", d), k2(f"eF{d}"), ALU.mult), S["G1_ev"])
                for d in (0, 1):
                    dve.wait_ge(S["G2_mm"], d + 1)
                    step(tt(NP[d], bk("a", d), k2(f"nP{d}"), ALU.mult), S["G2_ev"])
                for d in (0, 1):
                    dve.wait_ge(S["G3_mm"], d + 1)
                    step(tt(KF[d], bk("b", d), k2(f"sF{d}"), ALU.mult), S["G3_ev"])
                for d in (0, 1):
                    dve.wait_ge(S["G4_mm"], d + 1)
                    kl = k(f"iF{d}").unsqueeze(1).broadcast_to([P, NL, C])
                    step(tt(RB[d], bk("s", d)[:, 0:NL, :], kl, ALU.mult))
                    step(tt(RK[d], bk("s", d)[:, NL:NC, :], kl, ALU.mult), S["G4_ev"])
                for d in (0, 1):
                    for h in (0, 1):
                        eye = k("ident")[H[h], H[h]].unsqueeze(1).broadcast_to([C, NC, C])
                        step(tt(YY[d][H[h]], NF[d][H[h]], eye, ALU.add), S["y1_dn"] if h else None)
                step(tt(bo, KD[0][:, NTOK:T], KD[1][:, NTOK:T], ALU.add))
                step(stt(out=bo, in0=bo, scalar=c_("hrk"), in1=r_sh, op0=ALU.mult, op1=ALU.mult), S["bon_dn"])
                for job, b in (("Y2", "a"), ("Y4", "s"), ("Y8", "c"), ("Y16", "a")):
                    for d in (0, 1):
                        dve.wait_ge(S[f"{job}_mm"], d + 1)
                        step(tt(YY[d], YY[d], bk(b, d), ALU.add), S[f"{job}_ev"])
                for d in (0, 1):
                    dve.wait_ge(S["Y64_mm"], d + 1)
                    step(tt(YY[d], YY[d], bk("s", d), ALU.subtract), S["Y64_ev"])
                for i in range(NC):
                    for d in (0, 1):
                        c = order[d][i]
                        if i == 0:
                            dve.wait_ge(S["U0_ev"], d + 1)
                            step(ts(UN[d][:, c, :], U0[d][:, c, :], -1.0, None, ALU.mult), S[f"un_ev{d}"])
                        else:
                            dve.wait_ge(S[f"u_mm{d}"], i)
                            step(stt(out=UN[d][:, c, :], in0=PS[:, bank["a"][d], 0:C], scalar=-1.0, in1=U0[d][:, c, :],
                                     op0=ALU.mult, op1=ALU.subtract), S[f"un_ev{d}"])
                    if i == NC - 1:
                        break
                    for d in (0, 1):
                        c = order[d][i]
                        pc = PC[d][:, c:c + 1]
                        if i > 0:
                            step(ts(SP_[d], SS[d][:, i - 1, :], pc, None, ALU.mult))
                        dve.wait_ge(S[f"s_mm{d}"], i + 1)
                        sp = PS[:, bank["b"][d], 0:C]
                        if i == 0:
                            step(ts(SS[d][:, 0, :], sp, pc, None, ALU.mult), S[f"s_ev{d}"])
                        else:
                            step(stt(out=SS[d][:, i, :], in0=sp, scalar=pc, in1=SP_[d], op0=ALU.mult, op1=ALU.add), S[f"s_ev{d}"])
                dve.wait_ge(S["mean_mm"], 1)
                dve.wait_ge(S["y_ev"], 1)
                step(tt(yc, ys, PS[:, 1, 0:NTOK], ALU.subtract), S["yc_dn"])
                dve.wait_ge(S["bonus_mm"], 1)
                step(tt(bo, PS[:, 7, 0:NTOK], v_sh[:, NTOK:T], ALU.mult))
                dve.wait_ge(S["var_mm"], 1)
                step(ts(yq, PS[:, 2, 0:NTOK], GN_EPS, None, ALU.add), S["var_dn"])
                dve.wait_ge(S["std_ev"], 1)
                step(nc.vector.reciprocal(yq, yq))
                step(tt(yc, yc, yq, ALU.mult))
                step(ts(yc, yc, c_("ln_w"), c_("ln_b"), ALU.mult, ALU.add))
                step(tt(yc, yc, bo, ALU.add))
                step(tt(yc, yc, ZX[:, NTOK:T], ALU.mult))
                dve.wait_ge(S["conv_dn"], 1)
                step(tt(yc, yc, GAT[:, 0:NTOK], ALU.mult))
                nc.vector.tensor_tensor(MT[:, bass.ds(j, 1), :].rearrange("p o t -> p (o t)"), yc, cv, ALU.add).then_inc(iter_done, 1)
                dve.wait_ge(iter_go, j + 1)


SLOTS = 12
RAW, PARTS = 6, 4
ON_POOL = (0, 2, 6, 9)
NOSLOT = 1024.0


def project(nc, a, k, par, xl, MT, modT, npost, arena, PS, zw, cst, wout_loaded, f, pp, gg, rowv, count, **_):
    with ExitStack() as ctx:
        sem = ctx.enter_context(phase_semaphores(nc))
        r = Region(arena, NSLOT * KT * P, ARENA)
        wo = zw.rearrange("p s k c -> p (s k c)").rearrange("p (q n) -> p q n", n=D)
        rows = [r.take(D) for _ in range(3)] + [rowv[:, 0, :]]
        colv = r.take(4, KT)
        diag = r.take(4, P)
        diag2 = r.take(4, P)
        sq = r.take(D)
        st = r.take(2, 8)
        h2T = r.take(KT, P)
        wr = r.take(KT, NE)
        br = r.take(NE)
        lg, ex, sel, eq, cn = (r.take(TT, NE) for _ in range(5))
        m8 = r.take(TT, 8)
        gT = r.take(TT, P)
        bout = r.take(D)
        mxc = r.take(2)
        h2 = MT.rearrange("p k t -> p (k t)").rearrange("p (i n) -> p i n", n=D)
        names = ["in_small", "diag_dn", "rows_mm", "rows_ev", "mix_mm", "ss_ev", "ms_dn", "sd_ev", "x1_dn", "ss2_ev", "ms2_dn",
                 "sd2_ev", "h2_dn", "ht_mm", "ht_ev", "lg_mm", "negm_dn", "ex_ev", "sel_dn", "pos_mm", "g_dn", "gt_mm", "gt_ev",
                 "bias_mm", "dve_seq", "act_seq"]
        S = {n: sem("c_" + n) for n in names}
        block = ctx.enter_context(nc.Block())

        @block.sync
        def _(sp):
            sp.dma_start(wr, a["w_router"].rearrange("(q p) n -> p q n", p=P)).then_inc(S["in_small"], 16)
            sp.dma_start(br, a["b_router"].partition_broadcast(P)).then_inc(S["in_small"], 16)
            sp.dma_start(bout[0:NE, :], a["b_exp_out"]).then_inc(S["in_small"], 16)

        @block.tensor
        def _(pe):
            mm = nc.tensor.matmul
            pe.wait_ge(wout_loaded, 16)
            for i in range(TT):
                for kt in range(KT):
                    for n in range(2):
                        ins = mm(PS[:, 2 * i + n, :], MT[:, kt, i * P:(i + 1) * P], wo[:, kt, n * 512:(n + 1) * 512],
                                 start=kt == 0, stop=kt == KT - 1)
                ins.then_inc(S["mix_mm"], 1)
            for m in range(8):
                pe.wait_ge(S["diag_dn"], m + 1)
                if m >= 4:
                    pe.wait_ge(S["rows_ev"], m - 3)
                src = (diag if m % 2 == 0 else diag2).rearrange("p q n -> p (q n)")
                mm(PS[:, 4 + m % 4, :], k("ones"), src, start=True, stop=True).then_inc(S["rows_mm"], 1)
            pe.wait_ge(S["rows_ev"], 8)
            for i in range(TT):
                pe.wait_ge(S["h2_dn"], i + 1)
                if i:
                    pe.wait_ge(S["ht_ev"], 2 * i)
                for kt in range(KT):
                    ins = nc.tensor.transpose(PS[:, 4 + kt // 4, (kt % 4) * P:(kt % 4 + 1) * P], h2[:, i, kt * P:(kt + 1) * P], k("ident"))
                    if kt % 4 == 3:
                        ins.then_inc(S["ht_mm"], 1)
                pe.wait_ge(S["in_small"], 48)
                pe.wait_ge(S["ht_ev"], 2 * i + 2)
                for kt in range(KT):
                    ins = mm(PS[:, 6 + i, 0:NE], h2T[:, kt, :], wr[:, kt, :], start=kt == 0, stop=kt == KT - 1)
                ins.then_inc(S["lg_mm"], 1)
            pe.wait_ge(S["sel_dn"], 2)
            mm(PS[:, 4, 0:NE], k("before"), sel[:, 0, :], start=True, stop=True)
            for n, (w0, w1) in enumerate((("ones", "before"), ("ones", "ones"))):
                mm(PS[:, 4, NE * (n + 1):NE * (n + 2)], k(w0), sel[:, 0, :], start=True, stop=False)
                ins = mm(PS[:, 4, NE * (n + 1):NE * (n + 2)], k(w1), sel[:, 1, :], start=False, stop=True)
            ins.then_inc(S["pos_mm"], 1)
            pe.wait_ge(S["g_dn"], 1)
            for i in range(TT):
                ins = nc.tensor.transpose(PS[0:NE, 5, i * P:(i + 1) * P], gg[:, i, 0:NE], k("ident"))
            ins.then_inc(S["gt_mm"], 1)
            pe.wait_ge(S["gt_ev"], 1)
            for i in range(TT):
                for n in range(2):
                    ins = mm(PS[:, 2 * i + n, :], gT[0:NE, i, :], bout[0:NE, n * 512:(n + 1) * 512], start=True, stop=True)
            ins.then_inc(S["bias_mm"], 1)

        @block.scalar
        def _(act):
            A = nc.scalar.activation
            step = Steps(act, S["act_seq"])
            for i in range(TT):
                act.wait_ge(S["mix_mm"], i + 1)
                step(A(sq.rearrange("p (b n) -> p b n", b=2), PS[:, 2 * i:2 * i + 2, :], ACT.Square, accum_out=st[:, i, 0:1]), S["ss_ev"])
            for i in range(TT):
                act.wait_ge(S["ms_dn"], i + 1)
                step(A(st[:, i, 2:3], st[:, i, 1:2], ACT.Sqrt), S["sd_ev"])
            for m in range(8):
                act.wait_ge(S["rows_mm"], m + 1)
                step(A(rows[m // 2][:, (m % 2) * 512:(m % 2 + 1) * 512], PS[:, 4 + m % 4, :], ACT.Copy), S["rows_ev"])
            for i in range(TT):
                act.wait_ge(S["x1_dn"], i + 1)
                step(A(sq, xl[:, i, :], ACT.Square, accum_out=st[:, i, 3:4]), S["ss2_ev"])
            for i in range(TT):
                act.wait_ge(S["ms2_dn"], i + 1)
                step(A(st[:, i, 5:6], st[:, i, 4:5], ACT.Sqrt), S["sd2_ev"])
            for i in range(TT):
                for b in range(2):
                    act.wait_ge(S["ht_mm"], 2 * i + b + 1)
                    if i:
                        act.wait_ge(S["lg_mm"], i)
                    step(A(h2T[:, 4 * b:4 * b + 4, :], PS[:, 4 + b, :].rearrange("p (q n) -> p q n", n=P), ACT.Copy), S["ht_ev"])
            for i in range(TT):
                act.wait_ge(S["negm_dn"], i + 1)
                step(A(ex[:, i, :], lg[:, i, :], ACT.Exp, bias=st[:, i, 6:7]), S["ex_ev"])
            act.wait_ge(S["gt_mm"], 1)
            step(A(gT[0:NE], PS[0:NE, 5, 0:NTOK].rearrange("p (i n) -> p i n", n=P), ACT.Copy), S["gt_ev"])

        @block.vector
        def _(dve):
            tt, ts, stt = nc.vector.tensor_tensor, nc.vector.tensor_scalar, nc.vector.scalar_tensor_tensor
            step = Steps(dve, S["dve_seq"])
            mod = lambda i: modT[:, i * KT:(i + 1) * KT, 0]
            tt(colv[:, 0, :], mod(2), npost[:, 0, :], ALU.mult)
            stt(out=colv[:, 1, :], in0=mod(4), scalar=1.0, in1=npost[:, 1, :], op0=ALU.add, op1=ALU.mult)
            nc.vector.tensor_copy(colv[:, 2, :], mod(3))
            step(tt(colv[:, 3, :], mod(5), npost[:, 2, :], ALU.mult))
            for m in range(8):
                if m >= 2:
                    dve.wait_ge(S["rows_mm"], m - 1)
                dst = diag if m % 2 == 0 else diag2
                for q in range(4):
                    kt = (m % 2) * 4 + q
                    ins = ts(dst[:, q, :], k("ident"), colv[:, m // 2, kt:kt + 1], None, ALU.mult)
                ins.then_inc(S["diag_dn"], 1)
                if m == 1:
                    for i in range(TT):
                        dve.wait_ge(S["ss_ev"], i + 1)
                        step(ts(st[:, i, 1:2], st[:, i, 0:1], 1.0 / D, EPS, ALU.mult, ALU.add), S["ms_dn"])
            for i in range(TT):
                dve.wait_ge(S["sd_ev"], i + 1)
                step(nc.vector.reciprocal(st[:, i, 1:2], st[:, i, 2:3]))
            dve.wait_ge(S["rows_ev"], 8)
            for i in range(TT):
                two = lambda v: v.rearrange("p (b n) -> p b n", b=2)
                t = h2[:, i, :]
                step(stt(out=two(t), in0=PS[:, 2 * i:2 * i + 2, :], scalar=st[:, i, 1:2], in1=two(rows[0]), op0=ALU.mult, op1=ALU.mult))
                step(tt(xl[:, i, :], xl[:, i, :], t, ALU.add), S["x1_dn"])
            for i in range(TT):
                dve.wait_ge(S["ss2_ev"], i + 1)
                step(ts(st[:, i, 4:5], st[:, i, 3:4], 1.0 / D, EPS, ALU.mult, ALU.add), S["ms2_dn"])
            for i in range(TT):
                dve.wait_ge(S["sd2_ev"], i + 1)
                step(nc.vector.reciprocal(st[:, i, 4:5], st[:, i, 5:6]))
                step(stt(out=h2[:, i, :], in0=xl[:, i, :], scalar=st[:, i, 4:5], in1=rows[1], op0=ALU.mult, op1=ALU.mult))
                step(tt(h2[:, i, :], h2[:, i, :], rows[2], ALU.add), S["h2_dn"])
            dve.wait_ge(S["in_small"], 48)
            for i in range(TT):
                dve.wait_ge(S["lg_mm"], i + 1)
                step(tt(lg[:, i, :], PS[:, 6 + i, 0:NE], br, ALU.add))
                step(nc.vector.max(m8[:, i, :], lg[:, i, :]))
                step(ts(st[:, i, 6:7], m8[:, i, 0:1], -1.0, None, ALU.mult), S["negm_dn"])
                fourth = m8[:, i, TOPK - 1:TOPK]
                step(ts(eq[:, i, :], lg[:, i, :], fourth, None, ALU.is_equal))
                step(ts(sel[:, i, :], lg[:, i, :], fourth, None, ALU.is_gt))
                step(nc.vector.tensor_tensor_scan(cn[:, i, :], k("ones")[:, 0:NE], eq[:, i, :], 0.0, ALU.mult, ALU.add))
                step(nc.vector.reduce_sum(st[:, i, 7:8], sel[:, i, :], axis=AX))
                step(ts(cn[:, i, :], cn[:, i, :], st[:, i, 7:8], float(TOPK), ALU.add, ALU.is_le))
                step(tt(eq[:, i, :], eq[:, i, :], cn[:, i, :], ALU.mult))
                step(tt(sel[:, i, :], sel[:, i, :], eq[:, i, :], ALU.add), S["sel_dn"])
            step(nc.vector.memset(gg[:, :, :], 0.0))
            step(nc.vector.memset(pp[:, :, :], NOSLOT))
            for i in range(TT):
                dve.wait_ge(S["ex_ev"], i + 1)
                step(tt(ex[:, i, :], ex[:, i, :], sel[:, i, :], ALU.mult))
                step(nc.vector.reduce_sum(st[:, i, 7:8], ex[:, i, :], axis=AX))
                step(nc.vector.reciprocal(st[:, i, 7:8], st[:, i, 7:8]))
                for half in range(2):
                    step(ts(gg[:, i, half * NE:(half + 1) * NE], ex[:, i, :], st[:, i, 7:8], None, ALU.mult),
                         S["g_dn"] if (i, half) == (TT - 1, 1) else None)
            dve.wait_ge(S["pos_mm"], 1)
            for i in range(TT):
                p0, p1 = pp[:, i, 0:NE], pp[:, i, NE:2 * NE]
                step(stt(out=p0, in0=PS[:, 4, i * NE:(i + 1) * NE], scalar=-NOSLOT, in1=sel[:, i, :], op0=ALU.add, op1=ALU.mult))
                step(ts(p0, p0, NOSLOT, None, ALU.add))
                step(ts(p1, p0, -float(P), None, ALU.add))
            step(nc.vector.reduce_max(mxc[:, 0:1], PS[:, 4, 2 * NE:3 * NE], axis=AX))
            step(ts(mxc[:, 0:1], mxc[:, 0:1], float(P), float(NE), ALU.is_gt, ALU.mult))
            step(ts(mxc[:, 1:2], mxc[:, 0:1], float(NE), None, ALU.add))
            step(nc.vector.tensor_copy(count[:, :], mxc[:, 1:2]))
            dve.wait_ge(S["bias_mm"], 1)
            step(nc.vector.tensor_copy(f[:, :, :], PS[:, 0:4, :].rearrange("p (i b) n -> p i (b n)", i=TT)))


def experts(nc, a, k, xl, MT, PS, f, pp, gg, rowv, count, **_):
    with ExitStack() as ctx:
        sem = ctx.enter_context(phase_semaphores(nc))
        sb = lambda n, s, dt=F32: ctx.enter_context(nc.sbuf_tensor(n, s, dt))[tuple(slice(None) for _ in s)]
        f32 = lambda v: v.bitcast(F32)
        raw = sb("raw", [P, RAW, 2048])
        wh, wl = sb("wh", [P, PARTS, 2048], F32R), sb("wl", [P, PARTS, 2048], F32R)
        xh, xlow = sb("h2_high", [P, TT, D], F32R), sb("h2_low", [P, TT, D], F32R)
        hgh, hgl = sb("hg_high", [P, KT, P], F32R), sb("hg_low", [P, KT, P], F32R)
        aTh, aTl = sb("act_high", [P, KT, P], F32R), sb("act_low", [P, KT, P], F32R)
        take = sb("take", [P, TT, P], F32R)
        ye = sb("ye", [P, D])
        bias = sb("bias", [P, 2 * FF])
        back, backT = sb("back", [P, TT, P]), sb("backT", [P, TT, P])
        sg = sb("sg", [P, D])
        cur, curg = sb("cur", [P, TT, 2]), sb("curg", [P, TT, 2])
        st = sb("st", [P, 2, 4])
        h2 = MT.rearrange("p k t -> p (k t)").rearrange("p (i n) -> p i n", n=D)
        gs, us = h2[:, 0, :], h2[:, 1, :]
        raw_in = [sem(f"e_raw_in{q}") for q in range(RAW)]
        hi_dn = [sem(f"e_hi_dn{q}") for q in range(PARTS)]
        split_dn = [sem(f"e_split_dn{q}") for q in range(PARTS)]
        w_used = [sem(f"e_used{q}") for q in range(PARTS)]
        names = ["bias_in", "cleared", "sc_mm", "f_dn", "take_dn", "back_dn", "bt_mm", "bt_ev", "ga_mm", "hg_ev", "hg_dn",
                 "gate_dn", "gu_dn", "sig_ev", "act_dn", "at_mm", "at_ev", "at_dn", "ye_ev", "ss_ev", "ms_dn", "sd_ev",
                 "out_dn", "out_in", "xh_ev", "x_dn", "dve_seq", "act_seq"]
        S = {n: sem("e_" + n) for n in names}
        two = lambda v: v.rearrange("p (b n) -> p b n", b=2)
        quarters = lambda b: PS[:, b, :].rearrange("p (q n) -> p q n", n=P)
        block = ctx.enter_context(nc.Block())
        load = lambda eng: eng.value_load(count[0:1, 0:1], min_val=NE, max_val=2 * NE)
        LAPS, RAW_LAPS = SLOTS // PARTS, SLOTS // RAW
        lap = lambda i, s: i * LAPS + s // PARTS
        AHEAD = PARTS
        ACT_BANK = (4, 1)

        def high(act, i, s):
            q = s % PARTS
            act.wait_ge(raw_in[s % RAW], (i * RAW_LAPS + s // RAW) * 32 + 32)
            act.wait_ge(w_used[q], lap(i, s) + 1)
            nc.scalar.activation(wh[:, q, :], raw[:, s % RAW, :], ACT.Copy).then_inc(hi_dn[q], 1)

        def low(eng, engine, i, s):
            q = s % PARTS
            eng.wait_ge(hi_dn[q], lap(i, s) + 1)
            engine.tensor_tensor(wl[:, q, :], raw[:, s % RAW, :], f32(wh[:, q, :]), ALU.subtract).then_inc(split_dn[q], 1)

        @block.sync
        def _(sp):
            n = load(sp)

            def fetch(i, s):
                if s < RAW:
                    sp.wait_ge(split_dn[(s + RAW) % PARTS], lap(i, s + RAW) + 1)
                else:
                    sp.wait_ge(split_dn[(s - RAW) % PARTS], lap(i, s - RAW) + LAPS + 1)
                e = 0 if isinstance(i, int) else i % NE
                if s < KT:
                    rows, cols, to = s % 4 * 2 * P, s // 4 * 512, two(raw[:, s % RAW, :])
                    for b in range(2):
                        src = a["w_exp_in"][bass.ds(e, 1), rows + b * P:rows + (b + 1) * P, :].rearrange("o p (g n) -> p (o g) n", g=2)
                        sp.dma_start(two(to[:, b, :]), src[:, :, cols:cols + 512]).then_inc(raw_in[s % RAW], 16)
                else:
                    for b in range(2):
                        rows = ((s - KT) * 2 + b) * P
                        src = a["w_exp_out"][bass.ds(e, 1), rows:rows + P, :].rearrange("o p n -> p (o n)")
                        sp.dma_start(raw[:, s % RAW, b * D:(b + 1) * D], src).then_inc(raw_in[s % RAW], 16)

            for s in range(AHEAD):
                fetch(0, s)
            with sp.Fori(0, n) as i:
                for s in range(AHEAD, SLOTS):
                    fetch(i, s)
                    if s == AHEAD + 1:
                        sp.wait_ge(S["gu_dn"], i * 2 + 2)
                        sp.dma_start(bias, a["b_exp_in"][bass.ds(i % NE, 1), :].rearrange("o n -> (o n)").partition_broadcast(P)).then_inc(S["bias_in"], 16)
                for s in range(AHEAD):
                    fetch(i + 1, s)
            sp.wait_ge(S["out_dn"], TT)
            for i in range(TT):
                sp.dma_start(a["out"][i * P:(i + 1) * P, :], h2[:, i, :]).then_inc(S["out_in"], 16)
            sp.wait_ge(S["out_in"], 16 * TT)

        @block.gpsimd
        def _(pool):
            n = load(pool)
            for s in range(AHEAD):
                if s in ON_POOL:
                    low(pool, nc.gpsimd, 0, s)
            with pool.Fori(0, n) as i:
                for s in range(AHEAD, SLOTS + AHEAD):
                    if s % SLOTS in ON_POOL:
                        low(pool, nc.gpsimd, i + s // SLOTS, s % SLOTS)

        @block.tensor
        def _(pe):
            mm = nc.tensor.matmul
            n = load(pe)

            def gather():
                for kt in range(KT):
                    for i in range(TT):
                        for part in (xh, xlow):
                            ins = mm(PS[:, kt // 4 * 2, (kt % 4) * P:(kt % 4 + 1) * P], part[:, i, kt * P:(kt + 1) * P], take[:, i, :],
                                     start=i == 0 and part is xh, stop=i == TT - 1 and part is xlow)
                    if kt % 4 == 3:
                        ins.then_inc(S["ga_mm"], 1)

            def product(out, xhigh, xlo, q, cols, first, last):
                for p, (x, w) in enumerate(((xhigh, wh), (xlo, wh), (xhigh, wl))):
                    for m, o in enumerate(out):
                        ins = mm(o, x, w[:, q, cols + m * 512:cols + (m + 1) * 512], start=first and p == 0, stop=last and p == 2)
                return ins

            def turn_back():
                for m in range(TT):
                    ins = nc.tensor.transpose(PS[:, 6, m * P:(m + 1) * P], back[:, m, :], k("ident"))
                ins.then_inc(S["bt_mm"], 1)

            def turn_act(i, half):
                pe.wait_ge(S["act_dn"], i * 2 + half + 1)
                for r in range(4):
                    ins = nc.tensor.transpose(PS[:, ACT_BANK[half], r * P:(r + 1) * P], gs[:, (4 * half + r) * P:(4 * half + r + 1) * P], k("ident"))
                ins.then_inc(S["at_mm"], 1)

            def scatter(i):
                for half in range(2):
                    ins = mm(PS[:, 6 + half, :], backT[:, i, :], ye[:, half * 512:(half + 1) * 512], start=True, stop=True)
                ins.then_inc(S["sc_mm"], 1)

            for q in range(PARTS):
                pe.sem_inc(w_used[q], 1)
                pe.sem_inc(split_dn[q], LAPS)
            pe.wait_ge(S["take_dn"], 1)
            pe.wait_ge(S["x_dn"], 1)
            gather()
            with pe.Fori(0, n) as i:
                for s in range(KT):
                    half, q = s // 4, s % PARTS
                    pe.wait_ge(split_dn[q], lap(i, s) + LAPS + 1)
                    if s == 0:
                        pe.wait_ge(S["cleared"], 1)
                        pe.wait_ge(S["hg_dn"], i * 2 + 2)
                    if s == 4:
                        pe.wait_ge(S["gu_dn"], i * 2 + 2)
                        pe.wait_ge(S["at_dn"], i * 2 + 2)
                    for b in range(2):
                        kt = s % 4 * 2 + b
                        ins = product([PS[:, half, :], PS[:, 2 + half, :]], hgh[:, kt, :], hgl[:, kt, :], q, b * 1024, kt == 0, kt == KT - 1)
                    ins.then_inc(w_used[q], 1)
                    if s == 0:
                        pe.wait_ge(S["back_dn"], i + 1)
                        pe.wait_ge(S["f_dn"], i * 2 + 1)
                        turn_back()
                    if s == 2:
                        pe.wait_ge(S["ye_ev"], i * 2 + 2)
                        pe.wait_ge(S["bt_ev"], i + 1)
                        scatter(0)
                    if s == 5:
                        turn_act(i, 0)
                pe.wait_ge(S["take_dn"], i + 2)
                pe.wait_ge(S["gu_dn"], i * 2 + 3)
                gather()
                for b in range(2):
                    if b == 1:
                        turn_act(i, 1)
                        pe.wait_ge(S["f_dn"], i * 2 + 2)
                        scatter(1)
                    pe.wait_ge(S["at_dn"], i * 2 + b + 3)
                    for r in range(4):
                        kt = 4 * b + r
                        s = KT + kt // 2
                        q = s % PARTS
                        if kt % 2 == 0:
                            pe.wait_ge(split_dn[q], lap(i, s) + LAPS + 1)
                        ins = product([PS[:, 4 + m, :] for m in range(2)], aTh[:, kt, :], aTl[:, kt, :], q, (kt % 2) * D, kt == 0, kt == KT - 1)
                        if kt % 2 == 1:
                            ins.then_inc(w_used[q], 1)
            pe.wait_ge(S["back_dn"], n + 1)
            pe.wait_ge(S["f_dn"], n * 2 + 1)
            turn_back()
            pe.wait_ge(S["ye_ev"], n * 2 + 2)
            pe.wait_ge(S["bt_ev"], n + 1)
            scatter(0)
            pe.wait_ge(S["f_dn"], n * 2 + 2)
            scatter(1)

        @block.scalar
        def _(act):
            A = nc.scalar.activation
            n = load(act)

            def hg_copy(base):
                for b in range(2):
                    act.wait_ge(S["ga_mm"], base + b + 1)
                    A(hgh[:, 4 * b:4 * b + 4, :], quarters(2 * b), ACT.Copy).then_inc(S["hg_ev"], 1)

            def sigmoid(i, half):
                act.wait_ge(S["gate_dn"], i * 2 + half + 1)
                hs = slice(half * 512, (half + 1) * 512)
                A(sg[:, hs], gs[:, hs], ACT.Sigmoid, scale=1.702).then_inc(S["sig_ev"], 1)

            def act_copy(i, half):
                act.wait_ge(S["at_mm"], i * 2 + half + 1)
                A(aTh[:, 4 * half:4 * half + 4, :], quarters(ACT_BANK[half]), ACT.Copy).then_inc(S["at_ev"], 1)

            act.sem_inc(S["ye_ev"], 2)
            A(xh, h2, ACT.Copy).then_inc(S["xh_ev"], 1)
            for s in range(AHEAD):
                high(act, 0, s)
                if s == 1:
                    hg_copy(0)
            with act.Fori(0, n) as i:
                high(act, i, 4)
                act.wait_ge(S["bt_mm"], i + 1)
                A(backT, PS[:, 6, 0:NTOK].rearrange("p (q n) -> p q n", n=P), ACT.Copy).then_inc(S["bt_ev"], 1)
                high(act, i, 5)
                high(act, i, 6)
                sigmoid(i, 0)
                high(act, i, 7)
                high(act, i, 8)
                act_copy(i, 0)
                high(act, i, 9)
                high(act, i, 10)
                sigmoid(i, 1)
                high(act, i, 11)
                hg_copy(i * 2 + 2)
                high(act, i + 1, 0)
                act_copy(i, 1)
                for s in range(1, AHEAD):
                    high(act, i + 1, s)
                act.wait_ge(w_used[PARTS - 1], lap(i, SLOTS - 1) + 2)
                act.wait_ge(S["sc_mm"], i * 2 + 2)
                for b in range(2):
                    A(ye[:, b * 512:(b + 1) * 512], PS[:, 4 + b, :], ACT.Copy).then_inc(S["ye_ev"], 1)
            act.wait_ge(S["bt_mm"], n + 1)
            A(backT, PS[:, 6, 0:NTOK].rearrange("p (q n) -> p q n", n=P), ACT.Copy).then_inc(S["bt_ev"], 1)
            step = Steps(act, S["act_seq"])
            for i in range(TT):
                act.wait_ge(S["f_dn"], n * 2 + 3)
                step(A(h2[:, i, :], f[:, i, :], ACT.Square, accum_out=st[:, i, 0:1]), S["ss_ev"])
            for i in range(TT):
                act.wait_ge(S["ms_dn"], i + 1)
                step(A(st[:, i, 2:3], st[:, i, 1:2], ACT.Sqrt), S["sd_ev"])

        @block.vector
        def _(dve):
            tt, ts, stt = nc.vector.tensor_tensor, nc.vector.tensor_scalar, nc.vector.scalar_tensor_tensor
            n = load(dve)
            step = Steps(dve, S["dve_seq"])

            def hg_low(base):
                for b in range(2):
                    dve.wait_ge(S["hg_ev"], base + b + 1)
                    part = slice(4 * b, 4 * b + 4)
                    tt(hgl[:, part, :], quarters(2 * b), f32(hgh[:, part, :]), ALU.subtract).then_inc(S["hg_dn"], 1)

            def add(m):
                tt(two(f[:, m, :]), two(f[:, m, :]), PS[:, 6:8, :], ALU.add).then_inc(S["f_dn"], 1)

            def lows(i, *slots):
                for s in slots:
                    if s not in ON_POOL:
                        low(dve, nc.vector, i, s)

            def gate_and_up(i, half):
                s = 4 * half + 3
                dve.wait_ge(w_used[s % PARTS], lap(i, s) + 2)
                if half == 0:
                    dve.wait_ge(S["at_dn"], i * 2 + 2)
                hs = slice(half * 512, (half + 1) * 512)
                step(tt(gs[:, hs], PS[:, half, :], bias[:, half * 512:(half + 1) * 512], ALU.add))
                ts(gs[:, hs], gs[:, hs], 7.0, None, ALU.min).then_inc(S["gate_dn"], 1)
                tt(us[:, hs], PS[:, 2 + half, :], bias[:, FF + half * 512:FF + (half + 1) * 512], ALU.add).then_inc(S["gu_dn"], 1)
                dve.wait_ge(S["gu_dn"], i * 2 + half + 3)
                step(ts(us[:, hs], us[:, hs], 7.0, -7.0, ALU.min, ALU.max))
                dve.wait_ge(S["sig_ev"], i * 2 + half + 1)
                step(stt(out=us[:, hs], in0=us[:, hs], scalar=1.0, in1=gs[:, hs], op0=ALU.add, op1=ALU.mult))
                tt(gs[:, hs], us[:, hs], sg[:, hs], ALU.mult).then_inc(S["act_dn"], 1)

            def act_low(i, half):
                dve.wait_ge(S["at_ev"], i * 2 + half + 1)
                part = slice(4 * half, 4 * half + 4)
                tt(aTl[:, part, :], quarters(ACT_BANK[half]), f32(aTh[:, part, :]), ALU.subtract).then_inc(S["at_dn"], 1)

            dve.wait_ge(S["xh_ev"], 1)
            tt(xlow, h2, f32(xh), ALU.subtract).then_inc(S["x_dn"], 1)
            nc.vector.memset(ye, 0.0)
            nc.vector.memset(back, 0.0).then_inc(S["cleared"], 1)
            step(nc.vector.tensor_copy(cur, pp[:, :, 0:2]))
            for m in range(TT):
                ins = ts(take[:, m, :], k("slots"), cur[:, m, 0:1], None, ALU.is_equal)
            ins.then_inc(S["take_dn"], 1)
            for s in range(AHEAD):
                if s not in ON_POOL:
                    low(dve, nc.vector, 0, s)
            hg_low(0)
            dve.wait_ge(S["cleared"], 1)
            dve.wait_ge(S["x_dn"], 1)
            dve.sem_clear(S["dve_seq"])
            dve.sem_inc(S["gu_dn"], 2)
            dve.sem_inc(S["at_dn"], 2)
            dve.sem_inc(S["f_dn"], 1)
            dve.sem_inc(S["back_dn"], 1)
            with dve.Fori(0, n) as i:
                step = Steps(dve, S["dve_seq"])
                lows(i, 4)
                dve.wait_ge(S["cleared"], 1)
                dve.wait_ge(S["take_dn"], i + 1)
                step(nc.vector.tensor_copy(cur, pp[:, :, bass.ds(i, 2)]))
                step(nc.vector.tensor_copy(curg, gg[:, :, bass.ds(i, 2)]))
                dve.wait_ge(S["bt_mm"], i + 1)
                for m in range(TT):
                    ins = ts(back[:, m, :], k("slots"), cur[:, m, 0:1], curg[:, m, 0:1], ALU.is_equal, ALU.mult)
                ins.then_inc(S["back_dn"], 1)
                dve.wait_ge(S["ga_mm"], i * 2 + 2)
                for m in range(TT):
                    ins = ts(take[:, m, :], k("slots"), cur[:, m, 1:2], None, ALU.is_equal)
                ins.then_inc(S["take_dn"], 1)
                lows(i, 5, 6)
                dve.wait_ge(S["sc_mm"], i * 2 + 1)
                add(0)
                dve.wait_ge(S["bias_in"], i * 16 + 16)
                gate_and_up(i, 0)
                lows(i, 7, 8)
                act_low(i, 0)
                lows(i, 9, 10)
                gate_and_up(i, 1)
                hg_low(i * 2 + 2)
                lows(i, 11)
                act_low(i, 1)
                dve.wait_ge(S["sc_mm"], i * 2 + 2)
                add(1)
                lows(i + 1, 0, 1, 2, 3)
                dve.wait_ge(S["cleared"], 1)
                both_halves = dve.snap(i * 2 + 2)
                dve.wait_ge(S["act_dn"], both_halves)
                dve.sem_clear(S["dve_seq"])
            step = Steps(dve, S["dve_seq"])
            for m in range(TT):
                dve.wait_ge(S["sc_mm"], n * 2 + m + 1)
                add(m)
            for i in range(TT):
                dve.wait_ge(S["ss_ev"], i + 1)
                step(ts(st[:, i, 1:2], st[:, i, 0:1], 1.0 / D, EPS, ALU.mult, ALU.add), S["ms_dn"])
            for i in range(TT):
                dve.wait_ge(S["sd_ev"], i + 1)
                step(nc.vector.reciprocal(st[:, i, 1:2], st[:, i, 2:3]))
                step(stt(out=h2[:, i, :], in0=f[:, i, :], scalar=st[:, i, 1:2], in1=rowv[:, 0, :], op0=ALU.mult, op1=ALU.mult))
                step(tt(h2[:, i, :], h2[:, i, :], xl[:, i, :], ALU.add), S["out_dn"])


def layouts(inp):
    f = lambda n: np.asarray(inp[n])[0]
    cols = lambda v: v.reshape(-1, P).T
    w_in = f("w_in")
    offs = SHARED + [o + j * P for j in range(KT) for o in PER_TILE]
    blocks = np.stack([w_in[:, o:o + P].reshape(KT, P, P).transpose(1, 0, 2) for o in offs])
    mu = f("mu_shift")
    par = [mu[K_OFF:K_OFF + D], mu[V_OFF:V_OFF + D], mu[R_OFF:R_OFF + D], f("w0")[0], f("w0")[1], f("a0")[0], f("a0")[1],
           f("k_k"), f("k_a"), f("r_k").reshape(D), f("ln_x_w"), f("ln_x_b"), *f("conv_w"), f("norm_pre_mix")]
    ups = [f("w_decay_up").reshape(P, D), f("w_iclr_up").reshape(P, D), f("w_gate_up")]
    return {
        "x": f("x"), "ctx": f("ctx"), "w_ada": f("w_ada"), "w_out": f("w_out"),
        "cT": np.stack([cols(f("c")), cols(np.asarray(inp["c_ctx"]))], axis=2),
        "b_ada": cols(f("b_ada")),
        "par": np.stack([cols(v) for v in par], axis=1),
        "npost": np.stack([cols(f(n)) for n in ("norm_post_mix", "norm_pre_ffn", "norm_post_ffn")], axis=1),
        "mu_sh": np.stack([mu[o:o + P] for o in SHARED], axis=1),
        "w_blk": blocks.reshape(len(offs), P, KT, P),
        "lora_up": np.stack([u.reshape(P, KT, P) for u in ups], axis=2).transpose(1, 0, 2, 3),
        "w_router": f("w_router"), "b_router": f("b_router").reshape(1, NE),
        "w_exp_in": f("w_exp_in"), "b_exp_in": f("b_exp_in"), "w_exp_out": f("w_exp_out"), "b_exp_out": f("b_exp_out"),
        "consts": constants(),
    }


def kernel(**inputs):
    import numpy as _np
    import concourse.bacc as _bacc
    from concourse import mybir as _mybir
    from concourse.bass_utils import run_bass_kernel_spmd as _run

    nc = _bacc.Bacc("TRN2", target_bir_lowering=False, num_devices=1)
    arrays, args = {}, {}
    for name, v in layouts(inputs).items():
        v = _np.ascontiguousarray(v)
        arrays[f"in_{name}"] = v
        args[name] = nc.dram_tensor(f"in_{name}", v.shape, _mybir.dt.from_np(v.dtype), kind="ExternalInput").ap()
    args["out"] = nc.dram_tensor("out_x", (NTOK, D), F32, kind="ExternalOutput").ap()
    build(nc, args)
    r = _run(nc, [arrays], core_ids=[0])
    return r.results[0]["out_x"].reshape(1, NTOK, D)
```

```python
from contextlib import ExitStack, contextmanager

import numpy as np

import concourse.bass as bass
from concourse import mybir

F32 = mybir.dt.float32
F32R = mybir.dt.float32r
I32 = mybir.dt.int32
ALU = mybir.AluOpType
ACT = mybir.ActivationFunctionType
AX = mybir.AxisListType.X

P = 128
D = 1024
KT = D // P
NTOK = 256
T = 2 * NTOK
TT = NTOK // P
GRID_W = 64
C = 64
NC = T // C
NL = NC // 2
NE = 32
TOPK = 4
FF = D
LORA = 64
EPS = 1e-6
GN_EPS = 64e-5
BLK = 32
DECAY_C = -0.5 * float(np.exp(-0.5))
BIG = 1.0e6

K_OFF, V_OFF, DEC_OFF, ICL_OFF, R_OFF, GL_OFF = 0, 1024, 2048, 2176, 2304, 3328
GB_OFF, GC_OFF, XIN_OFF, GA_OFF, GBR_OFF = 3456, 4480, 5504, 6528, 7552
SHARED = [DEC_OFF, ICL_OFF, GL_OFF]
PER_TILE = [K_OFF, V_OFF, R_OFF, GA_OFF, GBR_OFF, GB_OFF, GC_OFF, XIN_OFF]
NSLOT = len(PER_TILE)

HOST_PAR = ["mu_k", "mu_v", "mu_r", "w0_0", "w0_1", "a0_0", "a0_1", "k_k", "k_a", "r_k", "ln_w", "ln_b",
            "cw0", "cw1", "cw2", "npm"]
DERIVED = ["hw0_0", "hw0_1", "ha0_0", "ha0_1", "hka", "omka", "hrk"]
MIX = ["om", "q0", "q1", "q2", "q3", "prev", "next"]
PAR = {n: i for i, n in enumerate(HOST_PAR + DERIVED + [f"{m}_{t}" for t in "kvr" for m in MIX])}
NHOST, NPAR = len(HOST_PAR), len(PAR)

CONST = {}
_n = 0
for _name, _w in (("ident", P), ("ones", P), ("heads", P), ("headmean", P), ("before", P), ("slots", P),
                  ("cls", 4), ("scan0", T), ("scan1", T),
                  *((f"{m}{d}", C) for d in (0, 1) for m in ("nF", "eF", "nP", "sF", "iF"))):
    CONST[_name] = (_n, _w)
    _n += _w
NCONST = _n


def constants():
    out = np.zeros((P, NCONST), np.float32)

    def put(name, a):
        o, w = CONST[name]
        out[:, o:o + w] = a

    p = np.arange(P)
    put("ident", np.eye(P))
    put("ones", 1.0)
    same = (p[:, None] // C == p[None] // C).astype(np.float32)
    put("heads", same)
    put("headmean", same / C)
    put("before", (p[:, None] < p[None]).astype(np.float32))
    put("slots", np.broadcast_to(p, (P, P)))
    put("cls", (p[:, None] % 4 == np.arange(4)).astype(np.float32))
    t = np.arange(T)
    put("scan0", (t % C != 0).astype(np.float32)[None])
    put("scan1", (t % C != C - 1).astype(np.float32)[None])
    s, u = (p % C)[:, None], np.arange(C)[None]
    block = s // BLK == u // BLK
    for d in (0, 1):
        later = u > s if d == 0 else u < s
        earlier = u < s if d == 0 else u > s
        put(f"nF{d}", -(later & block).astype(np.float32))
        put(f"eF{d}", (later & ~block).astype(np.float32))
        put(f"nP{d}", -(earlier & block).astype(np.float32))
        put(f"sF{d}", later.astype(np.float32))
        put(f"iF{d}", (later | (u == s)).astype(np.float32))
    return out


class Region:

    def __init__(self, tensor, start, end, more=None):
        self.tensor, self.at, self.end, self.more = tensor, start, end, more

    def take(self, *shape):
        n = int(np.prod(shape))
        if self.at + n > self.end and self.more is not None:
            return self.more.take(*shape)
        v = self.tensor[:, self.at:self.at + n]
        self.at += n
        assert self.at <= self.end, (self.at, self.end)
        if len(shape) == 2:
            v = v.rearrange("p (a b) -> p a b", b=shape[1])
        if len(shape) == 3:
            v = v.rearrange("p (a b c) -> p a b c", b=shape[1], c=shape[2])
        return v


@contextmanager
def phase_semaphores(nc):
    given = []

    def sem(name):
        given.append(nc.alloc_semaphore(name))
        return given[-1]

    yield sem
    nc.clear_and_free_semaphores(given)
    nc.all_engine_barrier()


class Steps:

    def __init__(self, eng, own):
        self.eng, self.own, self.count = eng, own, {}

    def __call__(self, ins, sem=None):
        sem = self.own if sem is None else sem
        self.count[sem.name] = self.count.get(sem.name, 0) + 1
        ins.then_inc(sem, 1)
        self.eng.wait_ge(sem, self.count[sem.name])


SLOTS = 12
RAW, PARTS = 6, 4
ON_POOL = (0, 2, 6, 9)

ARENA = 41 * 1024 + 768 - RAW * 2048


def build(nc, a):
    with ExitStack() as ctx:
        sb = lambda n, s, dt=F32: ctx.enter_context(nc.sbuf_tensor(n, s, dt))
        cst = sb("cst", [P, NCONST])
        par = sb("par", [P, NPAR, KT])
        xl = sb("xl", [P, TT, D])
        MT = sb("MT", [P, KT, NTOK])
        modT = sb("modT", [P, 48, 2])
        npost = sb("npost", [P, 3, KT])
        PS = ctx.enter_context(nc.psum_tensor("PS", [P, 8, 512], F32))
        zw_loaded = [ctx.enter_context(nc.semaphore(f"zw_loaded{s}")) for s in range(NSLOT)]
        lu_loaded = ctx.enter_context(nc.semaphore("lu_loaded"))
        wout_loaded = ctx.enter_context(nc.semaphore("wout_loaded"))
        k = lambda n: cst[:, CONST[n][0]:CONST[n][0] + CONST[n][1]]
        f = sb("f", [P, TT, D])
        pp, gg = sb("pp", [P, TT, 2 * NE + 2]), sb("gg", [P, TT, 2 * NE + 2])
        rowv = sb("rowv", [P, 1, D])
        count = sb("count", [P, 1], I32)
        shared = dict(f=f, pp=pp, gg=gg, rowv=rowv, count=count, nc=nc, a=a, k=k, par=par, xl=xl, MT=MT[:, :, :],
                      modT=modT, npost=npost, PS=PS, cst=cst,
                      zw_loaded=zw_loaded, lu_loaded=lu_loaded, wout_loaded=wout_loaded)
        raw = sb("raw", [P, RAW, 2048])[:, :, :]
        raw_in = [ctx.enter_context(nc.semaphore(f"raw_in{q}")) for q in range(RAW)]
        shared.update(raw=raw, raw_in=raw_in)
        with nc.sbuf_tensor("arena", [P, ARENA], F32) as arena:
            r = Region(arena, 0, ARENA)
            first = dict(arena=arena, zw=r.take(NSLOT, KT, P), hT=r.take(KT, T), free=r.at)
            adaln(**shared, **first)
            mixing(**shared, **first)
            project(**shared, **first)
        experts(**shared)


def adaln(nc, a, k, par, xl, modT, npost, raw, arena, PS, zw, hT, free, cst, zw_loaded, **_):
    with ExitStack() as ctx:
        sem = ctx.enter_context(phase_semaphores(nc))
        r = Region(arena, free, ARENA, Region(raw.rearrange("p q n -> p (q n)"), 0, RAW * 2048))
        w = r.take(KT, 2048)
        xc = r.take(TT, D)
        xn = r.take(2, D)
        sq = r.take(D)
        cT = r.take(KT, 2)
        csil = r.take(KT, 2)
        rows = r.take(2048)
        stat = r.take(4, 3)
        bada = r.take(48)
        tmp = r.take(KT, 2)
        scale = r.take(KT, 2)
        consts_in, small_in, x_in = sem("consts_in"), sem("small_in"), [sem(f"x_in{i}") for i in range(4)]
        ada_in = [sem(f"ada_in{i}") for i in range(KT)]
        ada_used = [sem(f"ada_used{i}") for i in range(KT)]
        silu_ready, rows_ev, cols_mm, cols_ev = (sem(n) for n in ("silu_ready", "rows_ev", "cols_mm", "cols_ev"))
        ss_ready, ms_ready, rms_ready, xn_ready, xt_mm, xt_ev = (sem(n) for n in ("ss_ready", "ms_ready", "rms_ready", "xn_ready", "xt_mm", "xt_ev"))
        sig_ready, turning, vec, act_seq = sem("sig_ready"), sem("turning"), sem("vec_steps"), sem("act_steps")
        block = ctx.enter_context(nc.Block())

        def tile_of(i):
            return xc[:, i, :] if i < TT else xl[:, i - TT, :]

        @block.sync
        def _(sp):
            sp.dma_start(cst[:, :], a["consts"]).then_inc(consts_in, 16)
            for i in range(4):
                src = a["ctx"] if i < TT else a["x"]
                t0 = (i % TT) * P
                sp.dma_start(tile_of(i), src[t0:t0 + P, :]).then_inc(x_in[i], 16)
            with sp.Fori(0, 3) as g:
                for kt in range(KT):
                    sp.wait_ge(ada_used[kt], g + 1)
                    sp.dma_start(w[:, kt, :], a["w_ada"][kt * P:(kt + 1) * P, bass.ds(g * 2048, 2048)]).then_inc(ada_in[kt], 16)
            for s in range(NSLOT):
                b = s if s < 3 else 3 + s
                sp.dma_start(zw[:, s, :, :], a["w_blk"][b]).then_inc(zw_loaded[s], 16)

        @block.gpsimd
        def _(pool):
            pool.dma_start(cT, a["cT"]).then_inc(small_in, 16)
            pool.dma_start(par[:, 0:NHOST, :], a["par"]).then_inc(small_in, 16)
            pool.dma_start(bada, a["b_ada"]).then_inc(small_in, 16)
            pool.dma_start(npost[:, :, :], a["npost"]).then_inc(small_in, 16)

        @block.scalar
        def _(act):
            step = Steps(act, act_seq)
            act.wait_ge(small_in, 64)
            step(nc.scalar.activation(tmp, cT, ACT.Sigmoid), sig_ready)
            for i in range(4):
                act.wait_ge(x_in[i], 16)
                step(nc.scalar.activation(sq, tile_of(i), ACT.Square, accum_out=stat[:, i, 0:1]), ss_ready)
            for i in range(4):
                act.wait_ge(ms_ready, 1 + i)
                step(nc.scalar.activation(stat[:, i, 2:3], stat[:, i, 1:2], ACT.Sqrt), rms_ready)
            act.sem_inc(rows_ev, 1)
            with act.Fori(0, 3) as g:
                act.wait_ge(ada_used[KT - 1], g + 2)
                act.wait_ge(cols_mm, g + 1)
                for n in range(4):
                    ins = nc.scalar.activation(rows[0:2, n * 512:(n + 1) * 512], PS[32 * n:32 * n + 2, n, :], ACT.Copy)
                ins.then_inc(rows_ev, 1)

        @block.tensor
        def _(pe):
            pe.wait_ge(consts_in, 16)
            for i in range(4):
                pe.wait_ge(xn_ready, i + 1)
                for kt in range(KT):
                    if kt % 4 == 0 and i > 0:
                        pe.wait_ge(xt_ev, 2 * (i - 1) + kt // 4 + 1)
                    ins = nc.tensor.transpose(PS[:, 4 + kt // 4, (kt % 4) * P:(kt % 4 + 1) * P],
                                              xn[:, i % 2, kt * P:(kt + 1) * P], k("ident"))
                    if kt % 4 == 3:
                        ins.then_inc(xt_mm, 1)
            pe.wait_ge(silu_ready, 1)
            pe.sem_inc(cols_mm, 1)
            for kt in range(KT):
                pe.sem_inc(ada_used[kt], 1)
            with pe.Fori(0, 3) as g:
                pe.wait_ge(rows_ev, g + 1)
                for kt in range(KT):
                    pe.wait_ge(ada_in[kt], g * 16 + 16)
                    pe.wait_ge(silu_ready, 1)
                    for n in range(4):
                        ins = nc.tensor.matmul(PS[32 * n:32 * n + 2, n, :], csil[:, kt, :], w[:, kt, n * 512:(n + 1) * 512],
                                               start=kt == 0, stop=kt == KT - 1)
                    ins.then_inc(ada_used[kt], 1)
                pe.wait_ge(rows_ev, g + 2)
                pe.wait_ge(cols_ev, g + 1)
                pe.sem_inc(turning, 1)
                for m in range(16):
                    ins = nc.tensor.transpose(PS[:, 6, 2 * m:2 * m + 2], rows[0:2, m * P:(m + 1) * P], k("ident")[0:2, 0:2])
                ins.then_inc(cols_mm, 1)

        @block.vector
        def _(dve):
            step = Steps(dve, vec)
            dve.wait_ge(small_in, 64)
            dve.wait_ge(consts_in, 16)
            dve.wait_ge(sig_ready, 1)
            nc.vector.tensor_tensor(csil, tmp, cT, ALU.mult).then_inc(silu_ready, 1)
            pp = lambda n: par[:, PAR[n], :]
            for n in ("w0_0", "w0_1", "a0_0", "a0_1"):
                nc.vector.tensor_scalar(pp("h" + n), pp(n), 0.5, None, ALU.mult)
            nc.vector.tensor_scalar(pp("hka"), pp("k_a"), 0.5, None, ALU.mult)
            nc.vector.tensor_scalar(pp("omka"), pp("k_a"), -0.5, 1.0, ALU.mult, ALU.add)
            step(nc.vector.tensor_scalar(pp("hrk"), pp("r_k"), 0.5, None, ALU.mult))
            for t in "kvr":
                mixing_weights(nc, step, k, lambda n: pp(f"{n}_{t}"), pp(f"mu_{t}"))
            for i in range(4):
                dve.wait_ge(ss_ready, i + 1)
            for i in range(4):
                ins = nc.vector.tensor_scalar(stat[:, i, 1:2], stat[:, i, 0:1], 1.0 / D, EPS, ALU.mult, ALU.add)
                ins.then_inc(ms_ready, 1)
            for i in range(4):
                dve.wait_ge(rms_ready, i + 1)
                step(nc.vector.reciprocal(stat[:, i, 1:2], stat[:, i, 2:3]))
                if i >= 2:
                    dve.wait_ge(xt_mm, 2 * (i - 1))
                nc.vector.tensor_scalar(xn[:, i % 2, :], tile_of(i), stat[:, i, 1:2], None, ALU.mult).then_inc(xn_ready, 1)
                for half in range(2):
                    dve.wait_ge(xt_mm, 2 * i + half + 1)
                    src = PS[:, 4 + half, :].rearrange("p (q t) -> p q t", t=P)
                    nc.vector.tensor_copy(hT[:, 4 * half:4 * half + 4, i * P:(i + 1) * P], src).then_inc(xt_ev, 1)
            dve.sem_inc(cols_ev, 1)
            with dve.Fori(0, 3) as g:
                dve.wait_ge(consts_in, 16)
                dve.wait_ge(cols_mm, g + 2)
                src = PS[:, 6, 0:32].rearrange("p (m s) -> p m s", s=2)
                nc.vector.tensor_copy(modT[:, bass.ds(g * 16, 16), :], src).then_inc(cols_ev, 1)
            dve.wait_ge(cols_ev, 4)
            step(nc.vector.tensor_tensor(modT[:, :, :], modT[:, :, :], bada.unsqueeze(2).broadcast_to([P, 48, 2]), ALU.add))
            for s in range(2):
                nc.vector.tensor_scalar(scale[:, :, s], modT[:, KT:2 * KT, s], 1.0, None, ALU.add)
            step(nc.vector.tensor_copy(stat[:, 0, 0:1], stat[:, 0, 1:2]))
            for s in range(2):
                ins = nc.vector.tensor_tensor(scale[:, :, s], scale[:, :, s], pp("npm"), ALU.mult)
            step(ins)
            dve.wait_ge(xt_ev, 8)
            for kt in range(KT):
                for s, t0 in ((1, 0), (0, NTOK)):
                    v = hT[:, kt, t0:t0 + NTOK]
                    ins = nc.vector.tensor_scalar(v, v, scale[:, kt, s:s + 1], modT[:, kt, s:s + 1], ALU.mult, ALU.add)
            step(ins)


def mixing_weights(nc, step, k, out, mu):
    for q in range(4):
        nc.vector.tensor_scalar(out(f"q{q}"), mu, k("cls")[:, q:q + 1], None, ALU.mult)
    step(nc.vector.tensor_scalar(out("om"), mu, -1.0, 1.0, ALU.mult, ALU.add))
    nc.vector.tensor_tensor(out("prev"), out("q0"), out("q2"), ALU.add)
    step(nc.vector.tensor_tensor(out("next"), out("q1"), out("q3"), ALU.add))


def qshift(nc, step, z, out, col, done, ctx_tokens=True):
    t0 = NTOK if ctx_tokens else 0
    add = lambda o, i, m, s=None: step(nc.vector.scalar_tensor_tensor(
        out=o, in0=i, scalar=col(m), in1=o, op0=ALU.mult, op1=ALU.add), s)
    if ctx_tokens:
        add(out[:, 1:NTOK], z[:, 0:NTOK - 1], "prev")
        add(out[:, 0:NTOK - 1], z[:, 1:NTOK], "next")
    rows = lambda v: v[:, t0:t0 + NTOK].rearrange("p (r w) -> p r w", w=GRID_W)
    o, i = rows(out), rows(z)
    add(o[:, :, 1:GRID_W], i[:, :, 0:GRID_W - 1], "q0")
    add(o[:, :, 0:GRID_W - 1], i[:, :, 1:GRID_W], "q1")
    add(out[:, t0 + GRID_W:t0 + NTOK], z[:, t0:t0 + NTOK - GRID_W], "q2")
    add(out[:, t0:t0 + NTOK - GRID_W], z[:, t0 + GRID_W:t0 + NTOK], "q3", done)


def mixing(nc, a, k, par, MT, raw, arena, PS, zw, hT, free, zw_loaded, lu_loaded, wout_loaded, **_):
    with ExitStack() as ctx:
        sem = ctx.enter_context(phase_semaphores(nc))
        r = Region(arena, free, ARENA, Region(raw.rearrange("p q n -> p (q n)"), 0, RAW * 2048))
        lu = r.take(3, P)
        mu_sh = r.take(3)
        mx = {m: r.take(3) for m in MIX}
        twT, laT, sgT = r.take(T), r.take(T), r.take(NTOK)
        pj = r.take(NPAR)
        k_sh, v_sh, r_sh = r.take(T), r.take(T), r.take(NTOK)
        TW, TA, CUM, E1, E2 = ([r.take(T) for d in (0, 1)] for _ in range(5))
        AL, BE, KA = ([r.take(NC, C) for d in (0, 1)] for _ in range(3))
        RH = [r.take(NL, C) for d in (0, 1)]
        KK, KD = r.take(T), [r.take(T) for d in (0, 1)]
        PC = [r.take(NC) for d in (0, 1)]
        AT, BT, KTK = ([r.take(NC, C) for d in (0, 1)] for _ in range(3))
        VT = r.take(NC, C)
        NF, NP, EF, KF = ([r.take(NC, C) for d in (0, 1)] for _ in range(4))
        RB, RK = ([r.take(NL, C) for d in (0, 1)] for _ in range(2))
        YY = [r.take(NC, C) for d in (0, 1)]
        SS = [r.take(NC - 1, C) for d in (0, 1)]
        SP_ = [r.take(C) for d in (0, 1)]
        GAT, ZB, ZX = r.take(T), r.take(T), r.take(T)
        ys, yc, yq, bo, cu, cv, ct = (r.take(NTOK) for _ in range(7))
        root = r.take(1)
        chunks = lambda v: v.rearrange("p (c t) -> p c t", t=C)
        Q0P, Q0F = [chunks(v) for v in TW], [chunks(v) for v in TA]
        Q1P, Q1F = [chunks(v) for v in CUM], [chunks(v) for v in E2]
        WT, X, U0, UN = NF, NP, AL, KA
        TP, ET = Q0P, Q0F

        iter_done, iter_go = sem("iter_done"), sem("iter_go")
        shared_mm, shared_om, shared_dn, lora_ready = (sem(n) for n in ("shared_mm", "shared_om", "shared_dn", "lora_ready"))
        mu_in, seq0, ahead_mm = sem("mu_in"), sem("dve_prelude"), sem("ahead_mm")
        first = sem("loop_sems_begin")
        names = ["pj_ready", "z_mm", "om_ev", "k_dn", "v_dn", "r_dn", "lora_mm", "tw_ev", "ta_ev", "sq_ev", "ssq_mm",
                 "ssq_dn", "nrm_ev", "cum_dn", "e_ev", "gate_mm", "r2_ev", "feat_dn", "vt_mm", "vt_ev", "bon_dn",
                 "y_mm", "y_ev", "mean_mm", "yc_dn", "yq_ev", "var_mm", "var_dn", "std_ev", "bonus_mm", "pool_seq",
                 "conv_dn", "kd_dn", "rk_dn", "all_passed", "dve_seq", "act_seq", "y1_dn"]
        names += [f"{n}{d}" for d in (0, 1) for n in ("u_mm", "un_ev", "s_mm", "s_ev")]
        JOBS = ["G1", "G2", "G3", "G4", "AT", "N2P", "N2F", "BT", "KT", "Y2", "N4P", "N4F", "Y4", "N8P", "N8F",
                "Y8", "N16P", "Y16", "TP", "X", "ET", "Y64", "WT", "U0"]
        names += [f"{j}_{w}" for j in JOBS for w in ("mm", "ev")]
        S = {n: sem(n) for n in names}
        loop_sems = range(first.num + 1, first.num + 1 + len(names))
        assert [S[n].num for n in names] == list(loop_sems)
        order = [list(range(NC)), list(range(NL - 1, -1, -1)) + list(range(NC - 1, NL - 1, -1))]
        H = [slice(C * h, C * h + C) for h in (0, 1)]
        bank = {"c": (0, 1), "a": (3, 5), "b": (4, 6)}
        SHARED_BANK, K_BANK, V_BANK, R_BANK = (0, 1, 3), 2, 7, 0
        bk = lambda n, d: PS[:, bank[n][d], :].rearrange("p (c t) -> p c t", t=C)
        k2 = lambda n: k(n).unsqueeze(1).broadcast_to([P, NC, C])
        c_ = lambda n: pj[:, PAR[n]:PAR[n] + 1]

        block = ctx.enter_context(nc.Block())

        @block.sync
        def _(sp):
            sp.dma_start(mu_sh, a["mu_sh"]).then_inc(mu_in, 16)
            sp.dma_start(lu, a["lora_up"][0]).then_inc(lu_loaded, 16)
            for s in range(3):
                sp.wait_ge(shared_mm, s + 1)
                sp.dma_start(zw[:, s, :, :], a["w_blk"][3 + s]).then_inc(zw_loaded[s], 16)
            for s in range(2):
                sp.wait_ge(ahead_mm, s + 1)
                sp.dma_start(zw[:, s, :, :], a["w_blk"][3 + NSLOT + s]).then_inc(zw_loaded[s], 16)

            def rows_of_wout(s):
                sp.dma_start(zw[:, s, :, :].rearrange("p k c -> p (k c)"), a["w_out"][s * P:(s + 1) * P, :]).then_inc(wout_loaded, 16)

            def body(j, more):
                def refill(s, tile):
                    sp.dma_start(zw[:, s, :, :], a["w_blk"][bass.ds(tile * NSLOT + (3 + s), 1)].rearrange("o p k c -> p (o k) c")).then_inc(zw_loaded[s], 16)
                for s in range(2, NSLOT):
                    sp.wait_ge(S["z_mm"], s - 1)
                    if more:
                        refill(s, j + 1)
                    else:
                        rows_of_wout(s)
                sp.wait_ge(S["gate_mm"], 1)
                if more:
                    sp.dma_start(lu, a["lora_up"][bass.ds(j + 1, 1)].rearrange("o p k c -> p (o k) c")).then_inc(lu_loaded, 16)
                for s in range(2):
                    sp.wait_ge(S["z_mm"], NSLOT - 1 + s)
                    if more:
                        refill(s, (j + 2) % KT)
                    else:
                        rows_of_wout(s)
                sp.sem_inc(iter_done, 1)
                sp.wait_ge(shared_mm, 3)
                sp.wait_ge(iter_go, j + 1)

            with sp.Fori(0, KT - 1) as j:
                body(j, True)
            body(KT - 1, False)

        @block.gpsimd
        def _(pool):
            with pool.Fori(0, KT) as j:
                step = Steps(pool, S["pool_seq"])
                pool.wait_ge(S["pj_ready"], 1)
                tt, ts = nc.gpsimd.tensor_tensor, nc.gpsimd.tensor_scalar
                pool.wait_ge(S["k_dn"], 1)
                for d in (0, 1):
                    pool.wait_ge(S["ta_ev"], d + 1)
                    step(ts(KD[d], TA[d], c_("hka"), c_("omka"), ALU.mult, ALU.add))
                    step(tt(KD[d], KD[d], k_sh, ALU.mult))
                    step(ts(TA[d], TA[d], 0.5, 0.5, ALU.mult, ALU.add), S["kd_dn"])
                pool.wait_ge(S["r2_ev"], 3)
                step(tt(cu, ZB[:, NTOK:T], ZX[:, 0:NTOK], ALU.mult))
                step(ts(cv, cu, c_("cw1"), 0.0, ALU.mult, ALU.add))
                step(ts(ct[:, 0:NTOK - 1], cu[:, 0:NTOK - 1], c_("cw0"), 0.0, ALU.mult, ALU.add))
                step(tt(cv[:, 1:NTOK], cv[:, 1:NTOK], ct[:, 0:NTOK - 1], ALU.add))
                step(ts(ct[:, 1:NTOK], cu[:, 1:NTOK], c_("cw2"), 0.0, ALU.mult, ALU.add))
                step(tt(cv[:, 0:NTOK - 1], cv[:, 0:NTOK - 1], ct[:, 1:NTOK], ALU.add))
                step(tt(cv, cv, ZB[:, 0:NTOK], ALU.mult))
                step(ts(GAT, GAT, 0.5, 0.5, ALU.mult, ALU.add))
                step(tt(GAT[:, 0:NTOK], GAT[:, 0:NTOK], ZX[:, NTOK:T], ALU.mult))
                step(tt(cv, cv, GAT[:, NTOK:T], ALU.mult), S["conv_dn"])
                pool.wait_ge(iter_done, j * 4 + 4)
                pool.sem_inc(S["all_passed"], 1)
                pool.wait_ge(S["all_passed"], 1)
                pool.sem_clear(loop_sems)
                pool.sem_inc(iter_go, 1)

        @block.scalar
        def _(act):
            A = nc.scalar.activation
            act.wait_ge(seq0, 1)
            for i, o in enumerate((twT, laT, sgT)):
                n = NTOK if i == 2 else T
                act.wait_ge(shared_mm, i + 1)
                A(o, PS[:, SHARED_BANK[i], 0:n], ACT.Copy, scale=mx["om"][:, i:i + 1]).then_inc(shared_om, 1)
            act.wait_ge(shared_dn, 1)
            A(twT, twT, ACT.Tanh).then_inc(lora_ready, 1)
            act.wait_ge(shared_dn, 3)
            A(sgT, sgT, ACT.Sigmoid).then_inc(lora_ready, 1)
            act.wait_ge(ahead_mm, 2)
            with act.Fori(0, KT) as j:
                step = Steps(act, S["act_seq"])
                act.wait_ge(S["pj_ready"], 1)
                for b, o, n, t in ((K_BANK, k_sh, T, "k"), (V_BANK, v_sh, T, "v"), (R_BANK, r_sh, NTOK, "r")):
                    if t == "r":
                        act.wait_ge(S["z_mm"], 1)
                    step(A(o, PS[:, b, 0:n], ACT.Copy, scale=c_(f"om_{t}")), S["om_ev"])
                act.wait_ge(S["k_dn"], 1)
                step(A(KK, k_sh, ACT.Square, scale=c_("k_k")), S["sq_ev"])
                for d in (0, 1):
                    act.wait_ge(S["lora_mm"], d + 1)
                    step(A(TW[d], PS[:, 3 + d, :], ACT.Tanh, scale=0.5, bias=c_(f"hw0_{d}")), S["tw_ev"])
                for d in (0, 1):
                    act.wait_ge(S["lora_mm"], d + 3)
                    step(A(TA[d], PS[:, 5 + d, :], ACT.Tanh, scale=0.5, bias=c_(f"ha0_{d}")), S["ta_ev"])
                for d in (0, 1):
                    act.wait_ge(S["cum_dn"], d + 1)
                    step(A(E1[d], CUM[d], ACT.Exp), S["e_ev"])
                    step(A(E2[d], CUM[d], ACT.Exp, scale=-1.0), S["e_ev"])
                act.wait_ge(S["ssq_dn"], 1)
                step(A(KK, KK, ACT.Sqrt), S["nrm_ev"])
                act.wait_ge(S["z_mm"], 3)
                step(A(GAT, PS[:, 1, :], ACT.Tanh, scale=0.5), S["r2_ev"])
                act.wait_ge(S["z_mm"], 5)
                step(A(ZB, PS[:, 3, :], ACT.Copy), S["r2_ev"])
                act.wait_ge(S["gate_mm"], 1)
                step(A(ZX, PS[:, 6, :], ACT.Copy), S["r2_ev"])

                def halves(job, out, d, b):
                    act.wait_ge(S[f"{job}_mm"], d + 1)
                    src = PS[:, b, :].rearrange("p (q n) -> p q n", n=P)
                    to = out.rearrange("p (q e) c -> p q e c", e=2)
                    for h in (0, 1):
                        for e in (0, 1):
                            ins = A(to[H[h], :, e, :], src[H[e], :, H[h]], ACT.Copy)
                            if (h, e) != (1, 1):
                                step(ins)
                    step(ins, S[f"{job}_ev"])

                def copy(job, out, d, b):
                    act.wait_ge(S[f"{job}_mm"], d + 1)
                    step(A(out[d], bk(b, d), ACT.Copy), S[f"{job}_ev"])

                halves("vt", VT, 0, bank["a"][0])
                for d in (0, 1):
                    halves("AT", AT[d], d, bank["a"][d])
                for d in (0, 1):
                    copy("N2P", Q0P, d, "b")
                for d in (0, 1):
                    copy("N2F", Q0F, d, "c")
                for job, out, b in (("BT", BT, "a"), ("KT", KTK, "b")):
                    for d in (0, 1):
                        halves(job, out[d], d, bank[b][d])
                for job, out, b in (("N4P", Q1P, "a"), ("N4F", Q1F, "b"), ("N8P", Q0P, "a"), ("N8F", Q0F, "b"),
                                    ("N16P", Q1P, "a"), ("TP", TP, "c"), ("X", X, "a"), ("ET", ET, "b"),
                                    ("WT", WT, "a"), ("U0", U0, "b")):
                    for d in (0, 1):
                        copy(job, out, d, b)
                step(A(root, k("ones")[:, 0:1], ACT.Sqrt))
                act.wait_ge(S["y_mm"], 1)
                step(A(ys, PS[:, 0, 0:NTOK], ACT.Copy), S["y_ev"])
                act.wait_ge(S["yc_dn"], 1)
                step(A(yq, yc, ACT.Square), S["yq_ev"])
                act.wait_ge(S["var_dn"], 1)
                step(A(yq, yq, ACT.Sqrt), S["std_ev"])
                act.sem_inc(iter_done, 1)
                act.wait_ge(iter_go, j + 1)

        @block.tensor
        def _(pe):
            mm = nc.tensor.matmul

            def zblock(slot, out, t0, N, signal):
                for kt in range(KT):
                    ins = mm(out, zw[:, slot, kt, :], hT[:, kt, t0:t0 + N], start=kt == 0, stop=kt == KT - 1)
                ins.then_inc(signal, 1)

            for s, (t0, N) in enumerate(((0, T), (0, T), (NTOK, NTOK))):
                pe.wait_ge(zw_loaded[s], 16)
                zblock(s, PS[:, SHARED_BANK[s], 0:N], t0, N, shared_mm)
            for s, b in enumerate((K_BANK, V_BANK)):
                pe.wait_ge(zw_loaded[s], 32)
                zblock(s, PS[:, b, :], 0, T, ahead_mm)
            pe.wait_ge(lora_ready, 2)
            pe.wait_ge(shared_dn, 3)
            with pe.Fori(0, KT) as j:
                pe.wait_ge(zw_loaded[2], j * 16 + 32)
                zblock(2, PS[:, R_BANK, 0:NTOK], NTOK, NTOK, S["z_mm"])
                pe.wait_ge(lu_loaded, j * 16 + 16)
                pe.wait_ge(shared_dn, 3)
                for i, src in enumerate((twT, laT)):
                    for d in (0, 1):
                        mm(PS[:, 3 + 2 * i + d, :], lu[H[d], i, :], src[H[d], :], start=True, stop=True).then_inc(S["lora_mm"], 1)
                pe.wait_ge(S["sq_ev"], 1)
                pe.wait_ge(S["k_dn"], 1)
                mm(PS[:, K_BANK, :], k("heads"), KK, start=True, stop=True).then_inc(S["ssq_mm"], 1)
                for i, s in enumerate((3, 4)):
                    pe.wait_ge(zw_loaded[s], j * 16 + 16)
                    zblock(s, PS[:, 1, i * NTOK:(i + 1) * NTOK], NTOK, NTOK, S["z_mm"])
                pe.wait_ge(S["tw_ev"], 2)
                for i, s in enumerate((5, 6)):
                    pe.wait_ge(zw_loaded[s], j * 16 + 16)
                    zblock(s, PS[:, 3, i * NTOK:(i + 1) * NTOK], NTOK, NTOK, S["z_mm"])

                def ahead(n):
                    s, half, kt = n // (2 * KT), n // KT % 2, n % KT
                    if n % (2 * KT) == 0:
                        pe.wait_ge(zw_loaded[s], j * 16 + 48)
                        pe.wait_ge(S["ssq_dn"] if s == 0 else S["v_dn"], 1)
                    cols = slice(half * NTOK, (half + 1) * NTOK)
                    ins = mm(PS[:, (K_BANK, V_BANK)[s], cols], zw[:, s, kt, :], hT[:, kt, cols], start=kt == 0, stop=kt == KT - 1)
                    if (kt, half) == (KT - 1, 1):
                        ins.then_inc(S["z_mm"], 1)

                def waits(d, *products):
                    for n in products:
                        pe.wait_ge(S[n], d + 1)

                def unit(job, b, d, lhsT, rhs):
                    out = bk(b, d)
                    for c in range(NC):
                        for h in (0, 1):
                            ins = mm(out[H[h], c, :], lhsT[H[h], c, :], rhs[H[h], c, :], start=True, stop=True)
                    ins.then_inc(S[f"{job}_mm"], 1)

                def turn(job, b, src):
                    for q in range(NC // 2):
                        ins = nc.tensor.transpose(PS[:, b, q * P:(q + 1) * P], src[:, 2 * q:2 * q + 2, :], k("ident"))
                    ins.then_inc(S[f"{job}_mm"], 1)

                pe.wait_ge(S["v_dn"], 1)
                pe.wait_ge(S["r2_ev"], 2)
                turn("vt", bank["a"][0], chunks(v_sh))
                pe.wait_ge(S["ta_ev"], 2)
                pe.wait_ge(S["r_dn"], 1)
                waits(0, "feat_dn")
                pe.wait_ge(zw_loaded[7], j * 16 + 16)
                zblock(7, PS[:, 6, 0:NTOK], NTOK, NTOK, S["z_mm"])
                mm(PS[:, 6, NTOK:T], lu[:, 2, :], sgT, start=True, stop=True).then_inc(S["gate_mm"], 1)
                for d in (0, 1):
                    waits(d, "feat_dn")
                    unit("G1", "c", d, BE[d], AL[d])
                    ahead(d)
                for d in (0, 1):
                    if d == 0:
                        pe.wait_ge(S["vt_ev"], 1)
                    unit("G2", "a", d, AL[d], BE[d])
                    ahead(2 + d)
                for d in (0, 1):
                    if d == 1:
                        pe.wait_ge(S["r2_ev"], 3)
                    unit("G3", "b", d, KA[d], AL[d])
                    ahead(4 + d)
                for d in (0, 1):
                    waits(d, "G1_ev")
                    out = bk("c", d)
                    for c in range(NL):
                        for h in (0, 1):
                            mm(out[H[h], c, :], BE[d][H[h], NL + c, :], RH[d][H[h], c, :], start=True, stop=True)
                            ins = mm(out[H[h], NL + c, :], KA[d][H[h], NL + c, :], RH[d][H[h], c, :], start=True, stop=True)
                    ins.then_inc(S["G4_mm"], 1)
                    if d == 0:
                        ahead(6)
                for d in (0, 1):
                    waits(d, "G2_ev")
                    turn("AT", bank["a"][d], AL[d])
                for d in (0, 1):
                    waits(d, "G3_ev")
                    unit("N2P", "b", d, NF[d], NP[d])
                    ahead(7 + d)
                for d in (0, 1):
                    waits(d, "G4_ev")
                    unit("N2F", "c", d, NP[d], NF[d])
                    if d == 0:
                        ahead(9)
                for job, b, src, before in (("BT", "a", BE, "AT_ev"), ("KT", "b", KA, "N2P_ev")):
                    for d in (0, 1):
                        waits(d, before)
                        turn(job, bank[b][d], src[d])
                for n, (job, b, lhsT, rhs, need) in enumerate((
                    ("Y2", "c", Q0P, YY, ("N2F_ev", "y1_dn")),
                    ("N4P", "a", Q0F, Q0P, ("BT_ev",)),
                    ("N4F", "b", Q0P, Q0F, ("KT_ev",)),
                    ("Y4", "c", Q1P, YY, ("N4P_ev", "Y2_ev")),
                    ("N8P", "a", Q1F, Q1P, ("N4F_ev",)),
                    ("N8F", "b", Q1P, Q1F, ()),
                    ("Y8", "c", Q0P, YY, ("N8P_ev", "Y4_ev")),
                    ("N16P", "a", Q0F, Q0P, ("N8F_ev",)),
                    ("Y16", "b", Q1P, YY, ("N16P_ev", "Y8_ev")),
                    ("TP", "c", YY, None, ("Y16_ev",)),
                    ("X", "a", KF, [VT, VT], ()),
                    ("ET", "b", EF, TP, ("TP_ev",)),
                    ("Y64", "c", ET, YY, ("ET_ev",)),
                    ("WT", "a", AT, YY, ("Y64_ev", "X_ev")),
                    ("U0", "b", YY, X, ()),
                )):
                    for d in (0, 1):
                        waits(d, *need)
                        if rhs is None:
                            out = bk(b, d)
                            for c in range(NC):
                                for h in (0, 1):
                                    ins = mm(out[H[h], c, :], lhsT[d][H[h], c, :], k("ident")[H[h], H[h]], start=True, stop=True)
                            ins.then_inc(S[f"{job}_mm"], 1)
                        else:
                            unit(job, b, d, lhsT[d], rhs[d])
                        m = 2 * n + d
                        if m % 4 < 3 and 10 + m - m // 4 < 4 * KT:
                            ahead(10 + m - m // 4)
                for d in (0, 1):
                    waits(d, "WT_ev", "U0_ev", "ET_ev")
                for i in range(NC):
                    for d in (0, 1):
                        c = order[d][i]
                        if i > 0:
                            pe.wait_ge(S[f"s_ev{d}"], i)
                            for h in (0, 1):
                                ins = mm(PS[H[h], bank["a"][d], 0:C], WT[d][H[h], c, :], SS[d][H[h], i - 1, :], start=True, stop=True)
                            ins.then_inc(S[f"u_mm{d}"], 1)
                    if i == NC - 1:
                        break
                    for d in (0, 1):
                        c = order[d][i]
                        pe.wait_ge(S[f"un_ev{d}"], i + 1)
                        for h in (0, 1):
                            out = PS[H[h], bank["b"][d], 0:C]
                            mm(out, BT[d][H[h], c, :], UN[d][H[h], c, :], start=True, stop=False)
                            ins = mm(out, KTK[d][H[h], c, :], VT[H[h], c, :], start=False, stop=True)
                        ins.then_inc(S[f"s_mm{d}"], 1)
                pe.wait_ge(S["bon_dn"], 1)
                pe.wait_ge(S["rk_dn"], 1)
                mm(PS[:, 4, 0:NTOK], k("heads"), bo, start=True, stop=True).then_inc(S["bonus_mm"], 1)
                for d in (0, 1):
                    pe.wait_ge(S[f"un_ev{d}"], NC)
                for c in range(NL):
                    for h in (0, 1):
                        out = PS[H[h], 0, c * C:(c + 1) * C]
                        for d in (0, 1):
                            i = order[d].index(NL + c)
                            mm(out, SS[d][H[h], i - 1, :], RH[d][H[h], c, :], start=d == 0, stop=False)
                            mm(out, UN[d][H[h], NL + c, :], RB[d][H[h], c, :], start=False, stop=False)
                        ins = mm(out, VT[H[h], NL + c, :], RK[0][H[h], c, :], start=False, stop=True)
                ins.then_inc(S["y_mm"], 1)
                pe.wait_ge(S["y_ev"], 1)
                mm(PS[:, 1, 0:NTOK], k("headmean"), ys, start=True, stop=True).then_inc(S["mean_mm"], 1)
                pe.wait_ge(S["yq_ev"], 1)
                mm(PS[:, 3, 0:NTOK], k("headmean"), yq, start=True, stop=True).then_inc(S["var_mm"], 1)
                pe.sem_inc(iter_done, 1)
                pe.wait_ge(iter_go, j + 1)

        @block.vector
        def _(dve):
            tt, ts, stt = nc.vector.tensor_tensor, nc.vector.tensor_scalar, nc.vector.scalar_tensor_tensor
            step = Steps(dve, seq0)
            dve.wait_ge(mu_in, 16)
            for q in range(4):
                ts(mx[f"q{q}"], mu_sh, k("cls")[:, q:q + 1], None, ALU.mult)
            step(ts(mx["om"], mu_sh, -1.0, 1.0, ALU.mult, ALU.add))
            tt(mx["prev"], mx["q0"], mx["q2"], ALU.add)
            step(tt(mx["next"], mx["q1"], mx["q3"], ALU.add))
            for i, o in enumerate((twT, laT, sgT)):
                n = NTOK if i == 2 else T
                dve.wait_ge(shared_om, i + 1)
                qshift(nc, step, PS[:, SHARED_BANK[i], 0:n], o, lambda m: mx[m][:, i:i + 1], shared_dn, i < 2)
            dve.wait_ge(lora_ready, 2)
            with dve.Fori(0, KT) as j:
                step = Steps(dve, S["dve_seq"])
                step(nc.vector.tensor_copy(pj, par[:, :, bass.ds(j, 1)].rearrange("p n o -> p (n o)")), S["pj_ready"])
                dve.wait_ge(S["om_ev"], 1)
                qshift(nc, step, PS[:, K_BANK, :], k_sh, lambda m: c_(m + "_k"), S["k_dn"])
                for d in (0, 1):
                    dve.wait_ge(S["tw_ev"], d + 1)
                    step(ts(TW[d], TW[d], DECAY_C, DECAY_C, ALU.mult, ALU.add))
                    o, w, m = CUM[d], TW[d], k(f"scan{d}")
                    if d == 1:
                        o, w, m = o[:, ::-1], w[:, ::-1], m[:, ::-1]
                    step(nc.vector.tensor_tensor_scan(o, m, w, 0.0, ALU.mult, ALU.add), S["cum_dn"])
                dve.wait_ge(S["om_ev"], 2)
                qshift(nc, step, PS[:, V_BANK, :], v_sh, lambda m: c_(m + "_v"), S["v_dn"])
                dve.wait_ge(S["ssq_mm"], 1)
                step(ts(KK, PS[:, K_BANK, :], 1e-24, None, ALU.max), S["ssq_dn"])
                dve.wait_ge(S["om_ev"], 3)
                qshift(nc, step, PS[:, R_BANK, 0:NTOK], r_sh, lambda m: c_(m + "_r"), S["r_dn"], False)
                dve.wait_ge(S["nrm_ev"], 1)
                dve.wait_ge(S["kd_dn"], 2)
                step(nc.vector.reciprocal(KK, KK))
                step(stt(out=KK, in0=k_sh, scalar=c_("k_k"), in1=KK, op0=ALU.mult, op1=ALU.mult))
                for d in (0, 1):
                    step(tt(TA[d], KK, TA[d], ALU.mult))
                    dve.wait_ge(S["e_ev"], 2 * d + 2)
                    e1, kk = chunks(E1[d]), chunks(KK)
                    step(tt(BE[d], chunks(TA[d]), chunks(E2[d]), ALU.mult))
                    step(tt(KA[d], chunks(KD[d]), chunks(E2[d]), ALU.mult))
                    ahead, behind = (slice(1, C), slice(0, C - 1)) if d == 0 else (slice(0, C - 1), slice(1, C))
                    edge, last = (0, C - 1) if d == 0 else (C - 1, 0)
                    step(tt(AL[d][:, :, ahead], kk[:, :, ahead], e1[:, :, behind], ALU.mult))
                    step(nc.vector.tensor_copy(AL[d][:, :, edge:edge + 1], kk[:, :, edge:edge + 1]))
                    step(tt(RH[d], chunks(r_sh), e1[:, NL:NC, :], ALU.mult))
                    step(nc.vector.tensor_copy(PC[d].unsqueeze(2), e1[:, :, last:last + 1]), S["feat_dn"])
                for d in (0, 1):
                    dve.wait_ge(S["G1_mm"], d + 1)
                    step(tt(NF[d], bk("c", d), k2(f"nF{d}"), ALU.mult))
                    step(tt(EF[d], bk("c", d), k2(f"eF{d}"), ALU.mult), S["G1_ev"])
                for d in (0, 1):
                    dve.wait_ge(S["G2_mm"], d + 1)
                    step(tt(NP[d], bk("a", d), k2(f"nP{d}"), ALU.mult), S["G2_ev"])
                for d in (0, 1):
                    dve.wait_ge(S["G3_mm"], d + 1)
                    step(tt(KF[d], bk("b", d), k2(f"sF{d}"), ALU.mult), S["G3_ev"])
                for d in (0, 1):
                    dve.wait_ge(S["G4_mm"], d + 1)
                    kl = k(f"iF{d}").unsqueeze(1).broadcast_to([P, NL, C])
                    step(tt(RB[d], bk("c", d)[:, 0:NL, :], kl, ALU.mult))
                    step(tt(RK[d], bk("c", d)[:, NL:NC, :], kl, ALU.mult), S["G4_ev"])
                for d in (0, 1):
                    for h in (0, 1):
                        eye = k("ident")[H[h], H[h]].unsqueeze(1).broadcast_to([C, NC, C])
                        step(tt(YY[d][H[h]], NF[d][H[h]], eye, ALU.add), S["y1_dn"] if h else None)
                step(tt(RK[0], RK[0], RK[1], ALU.add), S["rk_dn"])
                step(tt(bo, KD[0][:, NTOK:T], KD[1][:, NTOK:T], ALU.add))
                step(stt(out=bo, in0=bo, scalar=c_("hrk"), in1=r_sh, op0=ALU.mult, op1=ALU.mult), S["bon_dn"])
                for job, b in (("Y2", "c"), ("Y4", "c"), ("Y8", "c"), ("Y16", "b")):
                    for d in (0, 1):
                        dve.wait_ge(S[f"{job}_mm"], d + 1)
                        step(tt(YY[d], YY[d], bk(b, d), ALU.add), S[f"{job}_ev"])
                for d in (0, 1):
                    dve.wait_ge(S["Y64_mm"], d + 1)
                    step(tt(YY[d], YY[d], bk("c", d), ALU.subtract), S["Y64_ev"])
                for i in range(NC):
                    for d in (0, 1):
                        c = order[d][i]
                        if i == 0:
                            dve.wait_ge(S["U0_ev"], d + 1)
                            step(ts(UN[d][:, c, :], U0[d][:, c, :], -1.0, None, ALU.mult), S[f"un_ev{d}"])
                        else:
                            dve.wait_ge(S[f"u_mm{d}"], i)
                            step(stt(out=UN[d][:, c, :], in0=PS[:, bank["a"][d], 0:C], scalar=-1.0, in1=U0[d][:, c, :],
                                     op0=ALU.mult, op1=ALU.subtract), S[f"un_ev{d}"])
                    if i == NC - 1:
                        break
                    for d in (0, 1):
                        c = order[d][i]
                        pc = PC[d][:, c:c + 1]
                        if i > 0:
                            step(ts(SP_[d], SS[d][:, i - 1, :], pc, None, ALU.mult))
                        dve.wait_ge(S[f"s_mm{d}"], i + 1)
                        sp = PS[:, bank["b"][d], 0:C]
                        if i == 0:
                            step(ts(SS[d][:, 0, :], sp, pc, None, ALU.mult), S[f"s_ev{d}"])
                        else:
                            step(stt(out=SS[d][:, i, :], in0=sp, scalar=pc, in1=SP_[d], op0=ALU.mult, op1=ALU.add), S[f"s_ev{d}"])
                dve.wait_ge(S["mean_mm"], 1)
                dve.wait_ge(S["y_ev"], 1)
                step(tt(yc, ys, PS[:, 1, 0:NTOK], ALU.subtract), S["yc_dn"])
                dve.wait_ge(S["bonus_mm"], 1)
                step(tt(bo, PS[:, 4, 0:NTOK], v_sh[:, NTOK:T], ALU.mult))
                step(ts(bo, bo, c_("ln_b"), None, ALU.add))
                dve.wait_ge(S["var_mm"], 1)
                step(ts(yq, PS[:, 3, 0:NTOK], GN_EPS, None, ALU.add), S["var_dn"])
                dve.wait_ge(S["std_ev"], 1)
                step(nc.vector.reciprocal(yq, yq))
                step(tt(yc, yc, yq, ALU.mult))
                step(stt(out=yc, in0=yc, scalar=c_("ln_w"), in1=bo, op0=ALU.mult, op1=ALU.add))
                dve.wait_ge(S["conv_dn"], 1)
                step(tt(yc, yc, GAT[:, 0:NTOK], ALU.mult))
                nc.vector.tensor_tensor(MT[:, bass.ds(j, 1), :].rearrange("p o t -> p (o t)"), yc, cv, ALU.add).then_inc(iter_done, 1)
                dve.wait_ge(iter_go, j + 1)


NOSLOT = 1024.0


def project(nc, a, k, par, xl, MT, modT, npost, raw, raw_in, arena, PS, zw, cst, wout_loaded, f, pp, gg, rowv, count, **_):
    with ExitStack() as ctx:
        sem = ctx.enter_context(phase_semaphores(nc))
        r = Region(arena, NSLOT * KT * P, ARENA)
        wo = zw.rearrange("p s k c -> p (s k c)").rearrange("p (q n) -> p q n", n=D)
        rows = [r.take(D) for _ in range(3)] + [rowv[:, 0, :]]
        colv = r.take(4, KT)
        diag = r.take(4, P)
        diag2 = r.take(4, P)
        sq = r.take(D)
        st = r.take(2, 8)
        h2T = r.take(KT, P)
        wr = r.take(KT, NE)
        br = r.take(NE)
        lg, ex, sel, eq, cn = (r.take(TT, NE) for _ in range(5))
        m8 = r.take(TT, 8)
        gT = r.take(TT, P)
        bout = r.take(D)
        mxc = r.take(2)
        h2 = MT.rearrange("p k t -> p (k t)").rearrange("p (i n) -> p i n", n=D)
        names = ["in_small", "diag_dn", "rows_mm", "rows_ev", "mix_mm", "ss_ev", "ms_dn", "sd_ev", "x1_dn", "ss2_ev", "ms2_dn",
                 "sd2_ev", "h2_dn", "ht_mm", "ht_ev", "lg_mm", "negm_dn", "ex_ev", "sel_dn", "pos_mm", "g_dn", "gt_mm", "gt_ev",
                 "bias_mm", "dve_seq", "act_seq"]
        S = {n: sem("c_" + n) for n in names}
        block = ctx.enter_context(nc.Block())

        @block.sync
        def _(sp):
            sp.dma_start(wr, a["w_router"].rearrange("(q p) n -> p q n", p=P)).then_inc(S["in_small"], 16)
            sp.dma_start(br, a["b_router"].partition_broadcast(P)).then_inc(S["in_small"], 16)
            sp.dma_start(bout[0:NE, :], a["b_exp_out"]).then_inc(S["in_small"], 16)
            for s in range(PARTS):
                sp.dma_start(raw[:, s, :], a["w_exp"][s]).then_inc(raw_in[s], 16)

        @block.tensor
        def _(pe):
            mm = nc.tensor.matmul
            pe.wait_ge(wout_loaded, 16 * NSLOT)
            for i in range(TT):
                for kt in range(KT):
                    for n in range(2):
                        ins = mm(PS[:, 2 * i + n, :], MT[:, kt, i * P:(i + 1) * P], wo[:, kt, n * 512:(n + 1) * 512],
                                 start=kt == 0, stop=kt == KT - 1)
                ins.then_inc(S["mix_mm"], 1)
            for m in range(8):
                pe.wait_ge(S["diag_dn"], m + 1)
                if m >= 4:
                    pe.wait_ge(S["rows_ev"], m - 3)
                src = (diag if m % 2 == 0 else diag2).rearrange("p q n -> p (q n)")
                mm(PS[:, 4 + m % 4, :], k("ones"), src, start=True, stop=True).then_inc(S["rows_mm"], 1)
            pe.wait_ge(S["rows_ev"], 8)
            for i in range(TT):
                pe.wait_ge(S["h2_dn"], i + 1)
                if i:
                    pe.wait_ge(S["ht_ev"], 2 * i)
                for kt in range(KT):
                    ins = nc.tensor.transpose(PS[:, 4 + kt // 4, (kt % 4) * P:(kt % 4 + 1) * P], h2[:, i, kt * P:(kt + 1) * P], k("ident"))
                    if kt % 4 == 3:
                        ins.then_inc(S["ht_mm"], 1)
                pe.wait_ge(S["in_small"], 48)
                pe.wait_ge(S["ht_ev"], 2 * i + 2)
                for kt in range(KT):
                    ins = mm(PS[:, 6 + i, 0:NE], h2T[:, kt, :], wr[:, kt, :], start=kt == 0, stop=kt == KT - 1)
                ins.then_inc(S["lg_mm"], 1)
            pe.wait_ge(S["sel_dn"], 2)
            mm(PS[:, 4, 0:NE], k("before"), sel[:, 0, :], start=True, stop=True)
            for n, (w0, w1) in enumerate((("ones", "before"), ("ones", "ones"))):
                mm(PS[:, 4, NE * (n + 1):NE * (n + 2)], k(w0), sel[:, 0, :], start=True, stop=False)
                ins = mm(PS[:, 4, NE * (n + 1):NE * (n + 2)], k(w1), sel[:, 1, :], start=False, stop=True)
            ins.then_inc(S["pos_mm"], 1)
            pe.wait_ge(S["g_dn"], 1)
            for i in range(TT):
                ins = nc.tensor.transpose(PS[0:NE, 5, i * P:(i + 1) * P], gg[:, i, 0:NE], k("ident"))
            ins.then_inc(S["gt_mm"], 1)
            pe.wait_ge(S["gt_ev"], 1)
            for i in range(TT):
                for n in range(2):
                    ins = mm(PS[:, 2 * i + n, :], gT[0:NE, i, :], bout[0:NE, n * 512:(n + 1) * 512], start=True, stop=True)
            ins.then_inc(S["bias_mm"], 1)

        @block.scalar
        def _(act):
            A = nc.scalar.activation
            step = Steps(act, S["act_seq"])
            for i in range(TT):
                act.wait_ge(S["mix_mm"], i + 1)
                step(A(sq.rearrange("p (b n) -> p b n", b=2), PS[:, 2 * i:2 * i + 2, :], ACT.Square, accum_out=st[:, i, 0:1]), S["ss_ev"])
            for i in range(TT):
                act.wait_ge(S["ms_dn"], i + 1)
                step(A(st[:, i, 2:3], st[:, i, 1:2], ACT.Sqrt), S["sd_ev"])
            for m in range(8):
                act.wait_ge(S["rows_mm"], m + 1)
                step(A(rows[m // 2][:, (m % 2) * 512:(m % 2 + 1) * 512], PS[:, 4 + m % 4, :], ACT.Copy), S["rows_ev"])
            for i in range(TT):
                act.wait_ge(S["x1_dn"], i + 1)
                step(A(sq, xl[:, i, :], ACT.Square, accum_out=st[:, i, 3:4]), S["ss2_ev"])
            for i in range(TT):
                act.wait_ge(S["ms2_dn"], i + 1)
                step(A(st[:, i, 5:6], st[:, i, 4:5], ACT.Sqrt), S["sd2_ev"])
            for i in range(TT):
                for b in range(2):
                    act.wait_ge(S["ht_mm"], 2 * i + b + 1)
                    if i:
                        act.wait_ge(S["lg_mm"], i)
                    step(A(h2T[:, 4 * b:4 * b + 4, :], PS[:, 4 + b, :].rearrange("p (q n) -> p q n", n=P), ACT.Copy), S["ht_ev"])
            for i in range(TT):
                act.wait_ge(S["negm_dn"], i + 1)
                step(A(ex[:, i, :], lg[:, i, :], ACT.Exp, bias=st[:, i, 6:7]), S["ex_ev"])
            act.wait_ge(S["gt_mm"], 1)
            step(A(gT[0:NE], PS[0:NE, 5, 0:NTOK].rearrange("p (i n) -> p i n", n=P), ACT.Copy), S["gt_ev"])

        @block.vector
        def _(dve):
            tt, ts, stt = nc.vector.tensor_tensor, nc.vector.tensor_scalar, nc.vector.scalar_tensor_tensor
            step = Steps(dve, S["dve_seq"])
            mod = lambda i: modT[:, i * KT:(i + 1) * KT, 0]
            tt(colv[:, 0, :], mod(2), npost[:, 0, :], ALU.mult)
            stt(out=colv[:, 1, :], in0=mod(4), scalar=1.0, in1=npost[:, 1, :], op0=ALU.add, op1=ALU.mult)
            nc.vector.tensor_copy(colv[:, 2, :], mod(3))
            step(tt(colv[:, 3, :], mod(5), npost[:, 2, :], ALU.mult))
            for m in range(8):
                if m >= 2:
                    dve.wait_ge(S["rows_mm"], m - 1)
                dst = diag if m % 2 == 0 else diag2
                for q in range(4):
                    kt = (m % 2) * 4 + q
                    ins = ts(dst[:, q, :], k("ident"), colv[:, m // 2, kt:kt + 1], None, ALU.mult)
                ins.then_inc(S["diag_dn"], 1)
                if m == 1:
                    for i in range(TT):
                        dve.wait_ge(S["ss_ev"], i + 1)
                        step(ts(st[:, i, 1:2], st[:, i, 0:1], 1.0 / D, EPS, ALU.mult, ALU.add), S["ms_dn"])
            for i in range(TT):
                dve.wait_ge(S["sd_ev"], i + 1)
                step(nc.vector.reciprocal(st[:, i, 1:2], st[:, i, 2:3]))
            dve.wait_ge(S["rows_ev"], 8)
            for i in range(TT):
                two = lambda v: v.rearrange("p (b n) -> p b n", b=2)
                t = h2[:, i, :]
                step(stt(out=two(t), in0=PS[:, 2 * i:2 * i + 2, :], scalar=st[:, i, 1:2], in1=two(rows[0]), op0=ALU.mult, op1=ALU.mult))
                step(tt(xl[:, i, :], xl[:, i, :], t, ALU.add), S["x1_dn"])
            for i in range(TT):
                dve.wait_ge(S["ss2_ev"], i + 1)
                step(ts(st[:, i, 4:5], st[:, i, 3:4], 1.0 / D, EPS, ALU.mult, ALU.add), S["ms2_dn"])
            for i in range(TT):
                dve.wait_ge(S["sd2_ev"], i + 1)
                step(nc.vector.reciprocal(st[:, i, 4:5], st[:, i, 5:6]))
                step(stt(out=h2[:, i, :], in0=xl[:, i, :], scalar=st[:, i, 4:5], in1=rows[1], op0=ALU.mult, op1=ALU.mult))
                step(tt(h2[:, i, :], h2[:, i, :], rows[2], ALU.add), S["h2_dn"])
            dve.wait_ge(S["in_small"], 48)
            for i in range(TT):
                dve.wait_ge(S["lg_mm"], i + 1)
                step(tt(lg[:, i, :], PS[:, 6 + i, 0:NE], br, ALU.add))
                step(nc.vector.max(m8[:, i, :], lg[:, i, :]))
                step(ts(st[:, i, 6:7], m8[:, i, 0:1], -1.0, None, ALU.mult), S["negm_dn"])
                fourth = m8[:, i, TOPK - 1:TOPK]
                step(ts(eq[:, i, :], lg[:, i, :], fourth, None, ALU.is_equal))
                step(ts(sel[:, i, :], lg[:, i, :], fourth, None, ALU.is_gt))
                step(nc.vector.tensor_tensor_scan(cn[:, i, :], k("ones")[:, 0:NE], eq[:, i, :], 0.0, ALU.mult, ALU.add))
                step(nc.vector.reduce_sum(st[:, i, 7:8], sel[:, i, :], axis=AX))
                step(ts(cn[:, i, :], cn[:, i, :], st[:, i, 7:8], float(TOPK), ALU.add, ALU.is_le))
                step(tt(eq[:, i, :], eq[:, i, :], cn[:, i, :], ALU.mult))
                step(tt(sel[:, i, :], sel[:, i, :], eq[:, i, :], ALU.add), S["sel_dn"])
            step(nc.vector.memset(gg[:, :, :], 0.0))
            step(nc.vector.memset(pp[:, :, :], NOSLOT))
            for i in range(TT):
                dve.wait_ge(S["ex_ev"], i + 1)
                step(tt(ex[:, i, :], ex[:, i, :], sel[:, i, :], ALU.mult))
                step(nc.vector.reduce_sum(st[:, i, 7:8], ex[:, i, :], axis=AX))
                step(nc.vector.reciprocal(st[:, i, 7:8], st[:, i, 7:8]))
                for half in range(2):
                    step(ts(gg[:, i, half * NE:(half + 1) * NE], ex[:, i, :], st[:, i, 7:8], None, ALU.mult),
                         S["g_dn"] if (i, half) == (TT - 1, 1) else None)
            dve.wait_ge(S["pos_mm"], 1)
            for i in range(TT):
                p0, p1 = pp[:, i, 0:NE], pp[:, i, NE:2 * NE]
                step(stt(out=p0, in0=PS[:, 4, i * NE:(i + 1) * NE], scalar=-NOSLOT, in1=sel[:, i, :], op0=ALU.add, op1=ALU.mult))
                step(ts(p0, p0, NOSLOT, None, ALU.add))
                step(ts(p1, p0, -float(P), None, ALU.add))
            step(nc.vector.reduce_max(mxc[:, 0:1], PS[:, 4, 2 * NE:3 * NE], axis=AX))
            step(ts(mxc[:, 0:1], mxc[:, 0:1], float(P), float(NE), ALU.is_gt, ALU.mult))
            step(ts(mxc[:, 1:2], mxc[:, 0:1], float(NE), None, ALU.add))
            step(nc.vector.tensor_copy(count[:, :], mxc[:, 1:2]))
            dve.wait_ge(S["bias_mm"], 1)
            step(nc.vector.tensor_copy(f[:, :, :], PS[:, 0:4, :].rearrange("p (i b) n -> p i (b n)", i=TT)))


def experts(nc, a, k, xl, MT, raw, raw_in, PS, f, pp, gg, rowv, count, **_):
    with ExitStack() as ctx:
        sem = ctx.enter_context(phase_semaphores(nc))
        sb = lambda n, s, dt=F32: ctx.enter_context(nc.sbuf_tensor(n, s, dt))[tuple(slice(None) for _ in s)]
        f32 = lambda v: v.bitcast(F32)
        wh, wl = sb("wh", [P, PARTS, 2048], F32R), sb("wl", [P, PARTS, 2048], F32R)
        xh, xlow = sb("h2_high", [P, TT, D], F32R), sb("h2_low", [P, TT, D], F32R)
        hgh, hgl = sb("hg_high", [P, KT, P], F32R), sb("hg_low", [P, KT, P], F32R)
        aTh, aTl = sb("act_high", [P, KT, P], F32R), sb("act_low", [P, KT, P], F32R)
        take = sb("take", [P, TT, P], F32R)
        yh, yl = sb("y_high", [P, D], F32R), sb("y_low", [P, D], F32R)
        bias = sb("bias", [P, 2 * FF])
        back, backT = sb("back", [P, TT, P]), sb("backT", [P, TT, P], F32R)
        gate = sb("gate", [P, 1])
        sg = sb("sg", [P, D])
        cur, curg = sb("cur", [P, TT, 2]), sb("curg", [P, TT, 2])
        st = sb("st", [P, 2, 4])
        h2 = MT.rearrange("p k t -> p (k t)").rearrange("p (i n) -> p i n", n=D)
        gs, us = h2[:, 0, :], h2[:, 1, :]
        hi_dn = [sem(f"e_hi_dn{q}") for q in range(PARTS)]
        split_dn = [sem(f"e_split_dn{q}") for q in range(PARTS)]
        w_used = [sem(f"e_used{q}") for q in range(PARTS)]
        names = ["bias_in", "cleared", "sc_mm", "f_dn", "take_dn", "back_dn", "bt_mm", "bt_ev", "ga_mm", "hg_ev", "hg_dn",
                 "gate_dn", "gu_dn", "sig_ev", "act_dn", "at_mm", "at_ev", "at_dn", "y_dn", "gt_mm", "gt_ev", "yh_ev", "ss_ev", "ms_dn", "sd_ev",
                 "out_dn", "out_in", "xh_ev", "x_dn", "dve_seq", "act_seq"]
        S = {n: sem("e_" + n) for n in names}
        two = lambda v: v.rearrange("p (b n) -> p b n", b=2)
        quarters = lambda b: PS[:, b, :].rearrange("p (q n) -> p q n", n=P)
        block = ctx.enter_context(nc.Block())
        load = lambda eng: eng.value_load(count[0:1, 0:1], min_val=NE, max_val=2 * NE)
        LAPS, RAW_LAPS = SLOTS // PARTS, SLOTS // RAW
        lap = lambda i, s: i * LAPS + s // PARTS
        AHEAD = PARTS
        ACT_BANK = (4, 1)

        def high(act, i, s):
            q = s % PARTS
            act.wait_ge(raw_in[s % RAW], (i * RAW_LAPS + s // RAW) * 16 + 16)
            act.wait_ge(w_used[q], lap(i, s) + 1)
            nc.scalar.activation(wh[:, q, :], raw[:, s % RAW, :], ACT.Copy).then_inc(hi_dn[q], 1)

        def low(eng, engine, i, s):
            q = s % PARTS
            eng.wait_ge(hi_dn[q], lap(i, s) + 1)
            engine.tensor_tensor(wl[:, q, :], raw[:, s % RAW, :], f32(wh[:, q, :]), ALU.subtract).then_inc(split_dn[q], 1)

        @block.sync
        def _(sp):
            n = load(sp)

            def fetch(i, s):
                if s < RAW:
                    sp.wait_ge(split_dn[(s + RAW) % PARTS], lap(i, s + RAW) + 1)
                else:
                    sp.wait_ge(split_dn[(s - RAW) % PARTS], lap(i, s - RAW) + LAPS + 1)
                e = i % NE
                src = a["w_exp"][bass.ds(e * SLOTS + s, 1)].rearrange("o p n -> p (o n)")
                sp.dma_start(raw[:, s % RAW, :], src).then_inc(raw_in[s % RAW], 16)

            with sp.Fori(0, n) as i:
                for s in range(AHEAD, SLOTS):
                    fetch(i, s)
                    if s == AHEAD + 1:
                        sp.wait_ge(S["gu_dn"], i * 2 + 2)
                        sp.dma_start(bias, a["b_exp_in"][bass.ds(i % NE, 1), :].rearrange("o n -> (o n)").partition_broadcast(P)).then_inc(S["bias_in"], 16)
                for s in range(AHEAD):
                    fetch(i + 1, s)
            sp.wait_ge(S["out_dn"], TT)
            for i in range(TT):
                sp.dma_start(a["out"][i * P:(i + 1) * P, :], h2[:, i, :]).then_inc(S["out_in"], 16)
            sp.wait_ge(S["out_in"], 16 * TT)

        @block.gpsimd
        def _(pool):
            n = load(pool)
            for s in range(AHEAD):
                if s in ON_POOL:
                    low(pool, nc.gpsimd, 0, s)
            with pool.Fori(0, n) as i:
                for s in range(AHEAD, SLOTS + AHEAD):
                    if s % SLOTS in ON_POOL:
                        low(pool, nc.gpsimd, i + s // SLOTS, s % SLOTS)

        @block.tensor
        def _(pe):
            mm = nc.tensor.matmul
            n = load(pe)

            def gather():
                for kt in range(KT):
                    for i in range(TT):
                        for part in (xh, xlow):
                            ins = mm(PS[:, kt // 4 * 2, (kt % 4) * P:(kt % 4 + 1) * P], part[:, i, kt * P:(kt + 1) * P], take[:, i, :],
                                     start=i == 0 and part is xh, stop=i == TT - 1 and part is xlow)
                    if kt % 4 == 3:
                        ins.then_inc(S["ga_mm"], 1)

            def product(out, xhigh, xlo, q, cols, first, last):
                for p, (x, w) in enumerate(((xhigh, wh), (xlo, wh), (xhigh, wl))):
                    for m, o in enumerate(out):
                        ins = mm(o, x, w[:, q, cols + m * 512:cols + (m + 1) * 512], start=first and p == 0, stop=last and p == 2)
                return ins

            def turn_back():
                for m in range(TT):
                    ins = nc.tensor.transpose(PS[:, 6, m * P:(m + 1) * P], back[:, m, :], k("ident"))
                ins.then_inc(S["bt_mm"], 1)

            def turn_act(i, half):
                pe.wait_ge(S["act_dn"], i * 2 + half + 1)
                for r in range(4):
                    ins = nc.tensor.transpose(PS[:, ACT_BANK[half], r * P:(r + 1) * P], gs[:, (4 * half + r) * P:(4 * half + r + 1) * P], k("ident"))
                ins.then_inc(S["at_mm"], 1)

            def scatter(i):
                for part in (yh, yl):
                    for half in range(2):
                        ins = mm(PS[:, 6 + half, :], backT[:, i, :], part[:, half * 512:(half + 1) * 512], start=part is yh, stop=part is yl)
                ins.then_inc(S["sc_mm"], 1)

            for q in range(PARTS):
                pe.sem_inc(w_used[q], 1)
                pe.sem_inc(split_dn[q], LAPS)
            pe.wait_ge(S["take_dn"], 1)
            pe.wait_ge(S["x_dn"], 1)
            gather()
            with pe.Fori(0, n) as i:
                for s in range(KT):
                    half, q = s // 4, s % PARTS
                    pe.wait_ge(split_dn[q], lap(i, s) + LAPS + 1)
                    if s == 0:
                        pe.wait_ge(S["cleared"], 1)
                        pe.wait_ge(S["hg_dn"], i * 2 + 2)
                    if s == 4:
                        pe.wait_ge(S["gu_dn"], i * 2 + 2)
                        pe.wait_ge(S["at_dn"], i * 2 + 2)
                        pe.wait_ge(S["gt_ev"], i + 1)
                    for b in range(2):
                        kt = s % 4 * 2 + b
                        ins = product([PS[:, half, :], PS[:, 2 + half, :]], hgh[:, kt, :], hgl[:, kt, :], q, b * 1024, kt == 0, kt == KT - 1)
                    ins.then_inc(w_used[q], 1)
                    if s == 0:
                        pe.wait_ge(S["back_dn"], i + 1)
                        pe.wait_ge(S["f_dn"], i * 2 + 1)
                        turn_back()
                    if s == 2:
                        pe.wait_ge(S["y_dn"], i * 2 + 2)
                        pe.wait_ge(S["bt_ev"], i + 1)
                        scatter(0)
                    if s == 5:
                        turn_act(i, 0)
                pe.wait_ge(S["take_dn"], i + 2)
                pe.wait_ge(S["gu_dn"], i * 2 + 3)
                gather()
                for b in range(2):
                    if b == 1:
                        turn_act(i, 1)
                        pe.wait_ge(S["back_dn"], i + 2)
                        pe.wait_ge(S["gu_dn"], i * 2 + 4)
                        for m in range(TT):
                            ins = mm(PS[:, 3, 0:1], back[:, m, :], curg[:, m, 0:1], start=m == 0, stop=m == TT - 1)
                        ins.then_inc(S["gt_mm"], 1)
                        pe.wait_ge(S["f_dn"], i * 2 + 2)
                        scatter(1)
                    pe.wait_ge(S["at_dn"], i * 2 + b + 3)
                    for r in range(4):
                        kt = 4 * b + r
                        s = KT + kt // 2
                        q = s % PARTS
                        if kt % 2 == 0:
                            pe.wait_ge(split_dn[q], lap(i, s) + LAPS + 1)
                        ins = product([PS[:, 4 + m, :] for m in range(2)], aTh[:, kt, :], aTl[:, kt, :], q, (kt % 2) * D, kt == 0, kt == KT - 1)
                        if kt % 2 == 1:
                            ins.then_inc(w_used[q], 1)
            pe.wait_ge(S["back_dn"], n + 1)
            pe.wait_ge(S["f_dn"], n * 2 + 1)
            turn_back()
            pe.wait_ge(S["y_dn"], n * 2 + 2)
            pe.wait_ge(S["bt_ev"], n + 1)
            scatter(0)
            pe.wait_ge(S["f_dn"], n * 2 + 2)
            scatter(1)

        @block.scalar
        def _(act):
            A = nc.scalar.activation
            n = load(act)

            def hg_copy(base):
                for b in range(2):
                    act.wait_ge(S["ga_mm"], base + b + 1)
                    A(hgh[:, 4 * b:4 * b + 4, :], quarters(2 * b), ACT.Copy).then_inc(S["hg_ev"], 1)

            def sigmoid(i, half):
                act.wait_ge(S["gate_dn"], i * 2 + half + 1)
                hs = slice(half * 512, (half + 1) * 512)
                A(sg[:, hs], gs[:, hs], ACT.Sigmoid, scale=1.702).then_inc(S["sig_ev"], 1)

            def act_copy(i, half):
                act.wait_ge(S["at_mm"], i * 2 + half + 1)
                A(aTh[:, 4 * half:4 * half + 4, :], quarters(ACT_BANK[half]), ACT.Copy).then_inc(S["at_ev"], 1)

            act.sem_inc(S["gt_ev"], 1)
            A(xh, h2, ACT.Copy).then_inc(S["xh_ev"], 1)
            for s in range(AHEAD):
                high(act, 0, s)
                if s == 1:
                    hg_copy(0)
            with act.Fori(0, n) as i:
                high(act, i, 4)
                act.wait_ge(S["bt_mm"], i + 1)
                A(backT, PS[:, 6, 0:NTOK].rearrange("p (q n) -> p q n", n=P), ACT.Copy).then_inc(S["bt_ev"], 1)
                high(act, i, 5)
                high(act, i, 6)
                sigmoid(i, 0)
                high(act, i, 7)
                high(act, i, 8)
                act_copy(i, 0)
                high(act, i, 9)
                high(act, i, 10)
                sigmoid(i, 1)
                high(act, i, 11)
                hg_copy(i * 2 + 2)
                high(act, i + 1, 0)
                act_copy(i, 1)
                for s in range(1, AHEAD):
                    high(act, i + 1, s)
                act.wait_ge(S["y_dn"], i * 2 + 2)
                act.wait_ge(S["gt_mm"], i + 1)
                A(gate, PS[:, 3, 0:1], ACT.Copy).then_inc(S["gt_ev"], 1)
                act.wait_ge(w_used[PARTS - 1], lap(i, SLOTS - 1) + 2)
                act.wait_ge(S["sc_mm"], i * 2 + 2)
                act.wait_ge(S["gt_ev"], i + 2)
                for b in range(2):
                    A(yh[:, b * 512:(b + 1) * 512], PS[:, 4 + b, :], ACT.Copy, scale=gate[:, 0:1]).then_inc(S["yh_ev"], 1)
            act.wait_ge(S["bt_mm"], n + 1)
            A(backT, PS[:, 6, 0:NTOK].rearrange("p (q n) -> p q n", n=P), ACT.Copy).then_inc(S["bt_ev"], 1)
            step = Steps(act, S["act_seq"])
            for i in range(TT):
                act.wait_ge(S["f_dn"], n * 2 + 3)
                step(A(h2[:, i, :], f[:, i, :], ACT.Square, accum_out=st[:, i, 0:1]), S["ss_ev"])
            for i in range(TT):
                act.wait_ge(S["ms_dn"], i + 1)
                step(A(st[:, i, 2:3], st[:, i, 1:2], ACT.Sqrt), S["sd_ev"])

        @block.vector
        def _(dve):
            tt, ts, stt = nc.vector.tensor_tensor, nc.vector.tensor_scalar, nc.vector.scalar_tensor_tensor
            n = load(dve)
            step = Steps(dve, S["dve_seq"])

            def hg_low(base):
                for b in range(2):
                    dve.wait_ge(S["hg_ev"], base + b + 1)
                    part = slice(4 * b, 4 * b + 4)
                    tt(hgl[:, part, :], quarters(2 * b), f32(hgh[:, part, :]), ALU.subtract).then_inc(S["hg_dn"], 1)

            def add(m):
                tt(two(f[:, m, :]), two(f[:, m, :]), PS[:, 6:8, :], ALU.add).then_inc(S["f_dn"], 1)

            def lows(i, *slots):
                for s in slots:
                    if s not in ON_POOL:
                        low(dve, nc.vector, i, s)

            def gate_and_up(i, half):
                s = 4 * half + 3
                dve.wait_ge(w_used[s % PARTS], lap(i, s) + 2)
                if half == 0:
                    dve.wait_ge(S["at_dn"], i * 2 + 2)
                hs = slice(half * 512, (half + 1) * 512)
                step(tt(gs[:, hs], PS[:, half, :], bias[:, half * 512:(half + 1) * 512], ALU.add))
                ts(gs[:, hs], gs[:, hs], 7.0, None, ALU.min).then_inc(S["gate_dn"], 1)
                tt(us[:, hs], PS[:, 2 + half, :], bias[:, FF + half * 512:FF + (half + 1) * 512], ALU.add).then_inc(S["gu_dn"], 1)
                dve.wait_ge(S["gu_dn"], i * 2 + half + 3)
                step(ts(us[:, hs], us[:, hs], 7.0, -7.0, ALU.min, ALU.max))
                dve.wait_ge(S["sig_ev"], i * 2 + half + 1)
                step(stt(out=us[:, hs], in0=us[:, hs], scalar=1.0, in1=gs[:, hs], op0=ALU.add, op1=ALU.mult))
                tt(gs[:, hs], us[:, hs], sg[:, hs], ALU.mult).then_inc(S["act_dn"], 1)

            def act_low(i, half):
                dve.wait_ge(S["at_ev"], i * 2 + half + 1)
                part = slice(4 * half, 4 * half + 4)
                tt(aTl[:, part, :], quarters(ACT_BANK[half]), f32(aTh[:, part, :]), ALU.subtract).then_inc(S["at_dn"], 1)

            step(nc.vector.memset(sg, 0.0))
            nc.vector.tensor_copy(yh, sg)
            nc.vector.tensor_copy(yl, sg)
            nc.vector.memset(back, 0.0).then_inc(S["cleared"], 1)
            step(nc.vector.tensor_copy(cur, pp[:, :, 0:2]))
            for m in range(TT):
                ins = ts(take[:, m, :], k("slots"), cur[:, m, 0:1], None, ALU.is_equal)
            ins.then_inc(S["take_dn"], 1)
            dve.wait_ge(S["xh_ev"], 1)
            tt(xlow, h2, f32(xh), ALU.subtract).then_inc(S["x_dn"], 1)
            lows(0, 0, 1)
            hg_low(0)
            lows(0, 2, 3)
            dve.wait_ge(S["cleared"], 1)
            dve.wait_ge(S["x_dn"], 1)
            dve.sem_clear(S["dve_seq"])
            dve.sem_inc(S["gu_dn"], 2)
            dve.sem_inc(S["at_dn"], 2)
            dve.sem_inc(S["f_dn"], 1)
            dve.sem_inc(S["y_dn"], 2)
            dve.sem_inc(S["back_dn"], 1)
            with dve.Fori(0, n) as i:
                step = Steps(dve, S["dve_seq"])
                lows(i, 4)
                dve.wait_ge(S["cleared"], 1)
                dve.wait_ge(S["take_dn"], i + 1)
                step(nc.vector.tensor_copy(cur, pp[:, :, bass.ds(i, 2)]))
                dve.wait_ge(S["bt_mm"], i + 1)
                step(nc.vector.tensor_copy(curg, gg[:, :, bass.ds(i, 2)]))
                for m in range(TT):
                    ins = ts(back[:, m, :], k("slots"), cur[:, m, 0:1], None, ALU.is_equal)
                ins.then_inc(S["back_dn"], 1)
                dve.wait_ge(S["ga_mm"], i * 2 + 2)
                for m in range(TT):
                    ins = ts(take[:, m, :], k("slots"), cur[:, m, 1:2], None, ALU.is_equal)
                ins.then_inc(S["take_dn"], 1)
                lows(i, 5, 6)
                dve.wait_ge(S["sc_mm"], i * 2 + 1)
                add(0)
                dve.wait_ge(S["bias_in"], i * 16 + 16)
                gate_and_up(i, 0)
                lows(i, 7, 8)
                act_low(i, 0)
                lows(i, 9, 10)
                gate_and_up(i, 1)
                hg_low(i * 2 + 2)
                lows(i, 11)
                act_low(i, 1)
                dve.wait_ge(S["sc_mm"], i * 2 + 2)
                add(1)
                lows(i + 1, 0, 1, 2, 3)
                for b in range(2):
                    dve.wait_ge(S["yh_ev"], i * 2 + b + 1)
                    part = slice(b * 512, (b + 1) * 512)
                    stt(out=yl[:, part], in0=PS[:, 4 + b, :], scalar=gate[:, 0:1], in1=f32(yh[:, part]), op0=ALU.mult, op1=ALU.subtract).then_inc(S["y_dn"], 1)
                dve.wait_ge(S["cleared"], 1)
                both_halves = dve.snap(i * 2 + 2)
                dve.wait_ge(S["act_dn"], both_halves)
                dve.sem_clear(S["dve_seq"])
            step = Steps(dve, S["dve_seq"])
            for m in range(TT):
                dve.wait_ge(S["sc_mm"], n * 2 + m + 1)
                add(m)
            for i in range(TT):
                dve.wait_ge(S["ss_ev"], i + 1)
                step(ts(st[:, i, 1:2], st[:, i, 0:1], 1.0 / D, EPS, ALU.mult, ALU.add), S["ms_dn"])
            for i in range(TT):
                dve.wait_ge(S["sd_ev"], i + 1)
                step(nc.vector.reciprocal(st[:, i, 1:2], st[:, i, 2:3]))
                step(stt(out=h2[:, i, :], in0=f[:, i, :], scalar=st[:, i, 1:2], in1=rowv[:, 0, :], op0=ALU.mult, op1=ALU.mult))
                step(tt(h2[:, i, :], h2[:, i, :], xl[:, i, :], ALU.add), S["out_dn"])


def layouts(inp):
    f = lambda n: np.asarray(inp[n])[0]
    cols = lambda v: v.reshape(-1, P).T
    w_in = f("w_in")
    offs = SHARED + [o + j * P for j in range(KT) for o in PER_TILE]
    blocks = np.stack([w_in[:, o:o + P].reshape(KT, P, P).transpose(1, 0, 2) for o in offs])
    mu = f("mu_shift")
    par = [mu[K_OFF:K_OFF + D], mu[V_OFF:V_OFF + D], mu[R_OFF:R_OFF + D], f("w0")[0], f("w0")[1], f("a0")[0], f("a0")[1],
           f("k_k"), f("k_a"), f("r_k").reshape(D), f("ln_x_w"), f("ln_x_b"), *f("conv_w"), f("norm_pre_mix")]
    ups = [f("w_decay_up").reshape(P, D), f("w_iclr_up").reshape(P, D), f("w_gate_up")]
    into = f("w_exp_in").reshape(NE, 4, 2, P, 2, 2, 512).transpose(0, 5, 1, 3, 2, 4, 6).reshape(NE, KT, P, 2048)
    outof = f("w_exp_out").reshape(NE, 4, 2, P, D).transpose(0, 1, 3, 2, 4).reshape(NE, 4, P, 2048)
    slots = np.concatenate([into, outof], axis=1)
    return {
        "x": f("x"), "ctx": f("ctx"), "w_ada": f("w_ada"), "w_out": f("w_out"),
        "cT": np.stack([cols(f("c")), cols(np.asarray(inp["c_ctx"]))], axis=2),
        "b_ada": cols(f("b_ada")),
        "par": np.stack([cols(v) for v in par], axis=1),
        "npost": np.stack([cols(f(n)) for n in ("norm_post_mix", "norm_pre_ffn", "norm_post_ffn")], axis=1),
        "mu_sh": np.stack([mu[o:o + P] for o in SHARED], axis=1),
        "w_blk": blocks.reshape(len(offs), P, KT, P),
        "lora_up": np.stack([u.reshape(P, KT, P) for u in ups], axis=2).transpose(1, 0, 2, 3),
        "w_router": f("w_router"), "b_router": f("b_router").reshape(1, NE),
        "w_exp": slots.reshape(NE * SLOTS, P, 2048), "b_exp_in": f("b_exp_in"), "b_exp_out": f("b_exp_out"),
        "consts": constants(),
    }


def kernel(**inputs):
    import numpy as _np
    import concourse.bacc as _bacc
    from concourse import mybir as _mybir
    from concourse.bass_utils import run_bass_kernel_spmd as _run

    nc = _bacc.Bacc("TRN2", target_bir_lowering=False, num_devices=1)
    arrays, args = {}, {}
    for name, v in layouts(inputs).items():
        v = _np.ascontiguousarray(v)
        arrays[f"in_{name}"] = v
        args[name] = nc.dram_tensor(f"in_{name}", v.shape, _mybir.dt.from_np(v.dtype), kind="ExternalInput").ap()
    args["out"] = nc.dram_tensor("out_x", (NTOK, D), F32, kind="ExternalOutput").ap()
    build(nc, args)
    r = _run(nc, [arrays], core_ids=[0])
    return r.results[0]["out_x"].reshape(1, NTOK, D)
```
